# Optimizing a Trainium2 kernel written in Bass

```python
import jax, jax.numpy as jnp
from jax import lax
import numpy as np
import math

D_MODEL = 1024
BATCH = 1
SEQ = 512
DEPTH = 1

D_MIX = 2 * D_MODEL
D_ML = D_MIX // 2
N_ML_HEADS = 4
ML_HEAD_DIM = D_ML // N_ML_HEADS
QK_CONV = 4
ML_CHUNK = 128
D_CV = D_MIX - D_ML
CV_KERNEL = 31
N_IN = 2 * D_ML + D_ML + D_ML + 2 * N_ML_HEADS + 2 * D_CV
D_FF = ((8 * D_MODEL // 3 + 127) // 128) * 128
FFN_KERNEL = 3
N_MOD = 6
EPS = 1e-6


def rms_norm(x, g):
    xf = x.astype(jnp.float32)
    y = xf * lax.rsqrt(jnp.mean(xf * xf, axis=-1, keepdims=True) + EPS)
    return (y * g.astype(jnp.float32)).astype(x.dtype)

def layer_norm(x, g, b):
    xf = x.astype(jnp.float32)
    mu = jnp.mean(xf, axis=-1, keepdims=True)
    var = jnp.mean(jnp.square(xf - mu), axis=-1, keepdims=True)
    y = (xf - mu) * lax.rsqrt(var + EPS)
    return (y * g.astype(jnp.float32) + b.astype(jnp.float32)).astype(x.dtype)

def causal_dwconv(x, w, b):
    K, C = w.shape
    y = lax.conv_general_dilated(
        x, w[:, None, :].astype(x.dtype), window_strides=(1,), padding=[(K - 1, 0)],
        dimension_numbers=("NWC", "WIO", "NWC"), feature_group_count=C)
    return y + b

def mlstm_chunkwise(q, k, v, i_pre, f_pre):
    Bsz, S, H, Dh = q.shape
    L = ML_CHUNK
    nc = S // L

    def chunks(t):
        t = t.astype(jnp.float32).reshape((Bsz, nc, L, H) + t.shape[3:])
        return jnp.moveaxis(t, (1, 3), (0, 2))

    qc = chunks(q)
    kc = chunks(k) * (Dh ** -0.5)
    vc = chunks(v)
    ic = chunks(i_pre)
    lfc = jax.nn.log_sigmoid(chunks(f_pre))
    causal = jnp.tril(jnp.ones((L, L), dtype=bool))

    def step(carry, inp):
        C, n, m = carry
        q_, k_, v_, i_, lf_ = inp
        b = jnp.cumsum(lf_, axis=-1)
        dmat = jnp.where(causal, b[..., :, None] - b[..., None, :] + i_[..., None, :], -jnp.inf)
        m_t = jnp.maximum(b + m[..., None], jnp.max(dmat, axis=-1))
        w_inter = jnp.exp(b + m[..., None] - m_t)
        scores = jnp.einsum("bhtd,bhsd->bhts", q_, k_) * jnp.exp(dmat - m_t[..., None])
        num = (w_inter[..., None] * jnp.einsum("bhtd,bhde->bhte", q_, C)
               + jnp.einsum("bhts,bhse->bhte", scores, v_))
        den = w_inter * jnp.einsum("bhtd,bhd->bht", q_, n) + jnp.sum(scores, axis=-1)
        h = num / jnp.maximum(jnp.abs(den), jnp.exp(-m_t))[..., None]
        b_last = b[..., -1]
        g = b_last[..., None] - b + i_
        m_new = jnp.maximum(b_last + m, jnp.max(g, axis=-1))
        decay = jnp.exp(b_last + m - m_new)
        kw = k_ * jnp.exp(g - m_new[..., None])[..., None]
        C = decay[..., None, None] * C + jnp.einsum("bhsd,bhse->bhde", kw, v_)
        n = decay[..., None] * n + jnp.sum(kw, axis=2)
        return (C, n, m_new), h

    init = (jnp.zeros((Bsz, H, Dh, Dh), jnp.float32),
            jnp.zeros((Bsz, H, Dh), jnp.float32),
            jnp.zeros((Bsz, H), jnp.float32))
    _, h = lax.scan(step, init, (qc, kc, vc, ic, lfc))
    return jnp.moveaxis(h, (0, 2), (1, 3)).reshape(Bsz, S, H, Dh)

def first_inputs(seed: int = 0) -> dict:
    key = jax.random.key(seed)
    ks = jax.random.split(key, 24)

    def nrm(k, shape, scale):
        return jax.random.normal(k, shape, jnp.float32) * scale

    def gain(k, shape):
        return 1.0 + nrm(k, shape, 0.05)

    Ly = DEPTH
    fbias = jnp.linspace(3.0, 6.0, N_ML_HEADS, dtype=jnp.float32)[None, :] + nrm(ks[9], (Ly, N_ML_HEADS), 0.1)
    return {
        "x": nrm(ks[0], (BATCH, SEQ, D_MODEL), 1.0),
        "c": nrm(ks[1], (BATCH, D_MODEL), 1.0),
        "ada_w": nrm(ks[2], (Ly, D_MODEL, N_MOD * D_MODEL), 0.5 * D_MODEL ** -0.5),
        "ada_b": nrm(ks[3], (Ly, N_MOD * D_MODEL), 0.02),
        "mix_pre_g": gain(ks[4], (Ly, D_MODEL)),
        "mix_post_g": gain(ks[5], (Ly, D_MODEL)),
        "w_in": nrm(ks[6], (Ly, D_MODEL, N_IN), D_MODEL ** -0.5),
        "qk_conv_w": nrm(ks[7], (Ly, QK_CONV, 2 * D_ML), QK_CONV ** -0.5),
        "qk_conv_b": nrm(ks[8], (Ly, 2 * D_ML), 0.02),
        "igate_b": nrm(ks[10], (Ly, N_ML_HEADS), 0.1),
        "fgate_b": fbias,
        "ml_norm_g": gain(ks[11], (Ly, D_ML)),
        "cv_dw_w": nrm(ks[12], (Ly, CV_KERNEL, D_CV), CV_KERNEL ** -0.5),
        "cv_dw_b": nrm(ks[13], (Ly, D_CV), 0.02),
        "cv_ln_g": gain(ks[14], (Ly, D_CV)),
        "cv_ln_b": nrm(ks[15], (Ly, D_CV), 0.02),
        "w_out": nrm(ks[16], (Ly, D_MIX, D_MODEL), D_MIX ** -0.5),
        "ffn_pre_g": gain(ks[17], (Ly, D_MODEL)),
        "ffn_post_g": gain(ks[18], (Ly, D_MODEL)),
        "ffn_up": nrm(ks[19], (Ly, D_MODEL, 2 * D_FF), D_MODEL ** -0.5),
        "ffn_conv_w": nrm(ks[20], (Ly, FFN_KERNEL, 2 * D_FF), FFN_KERNEL ** -0.5),
        "ffn_conv_b": nrm(ks[21], (Ly, 2 * D_FF), 0.02),
        "ffn_down": nrm(ks[22], (Ly, D_FF, D_MODEL), D_FF ** -0.5),
    }

def first_block(x, c, ada_w, ada_b, mix_pre_g, mix_post_g, w_in, qk_conv_w, qk_conv_b,
              igate_b, fgate_b, ml_norm_g, cv_dw_w, cv_dw_b, cv_ln_g, cv_ln_b, w_out,
              ffn_pre_g, ffn_post_g, ffn_up, ffn_conv_w, ffn_conv_b, ffn_down):
    Bsz, S, _ = x.shape
    H, Dh = N_ML_HEADS, ML_HEAD_DIM
    cond = jax.nn.silu(c)
    for l in range(DEPTH):
        mod = cond @ ada_w[l] + ada_b[l]
        sh1, sc1, g1, sh2, sc2, g2 = jnp.split(mod[:, None, :], N_MOD, axis=-1)

        u = rms_norm(x, mix_pre_g[l]) * (1.0 + sc1) + sh1
        proj = u @ w_in[l]
        qk_raw, v, o_pre, gates, glu = jnp.split(
            proj, [2 * D_ML, 3 * D_ML, 4 * D_ML, 4 * D_ML + 2 * H], axis=-1)

        qk = jax.nn.silu(causal_dwconv(qk_raw, qk_conv_w[l], qk_conv_b[l]))
        q, k = jnp.split(qk, 2, axis=-1)
        heads = lambda t: t.reshape(Bsz, S, H, Dh)
        h = mlstm_chunkwise(heads(q), heads(k), heads(v),
                            gates[..., :H] + igate_b[l], gates[..., H:] + fgate_b[l])
        h = rms_norm(h, ml_norm_g[l].reshape(H, Dh)).reshape(Bsz, S, D_ML)
        h = (h * jax.nn.sigmoid(o_pre.astype(jnp.float32))).astype(x.dtype)

        a, gt = jnp.split(glu, 2, axis=-1)
        y = causal_dwconv(a * jax.nn.sigmoid(gt), cv_dw_w[l], cv_dw_b[l])
        y = jax.nn.silu(layer_norm(y, cv_ln_g[l], cv_ln_b[l]))

        mix = jnp.concatenate([h, y], axis=-1) @ w_out[l]
        x = x + g1 * rms_norm(mix, mix_post_g[l])

        u = rms_norm(x, ffn_pre_g[l]) * (1.0 + sc2) + sh2
        up = causal_dwconv(u @ ffn_up[l], ffn_conv_w[l], ffn_conv_b[l])
        a, gt = jnp.split(up, 2, axis=-1)
        f = (jax.nn.silu(gt) * a) @ ffn_down[l]
        x = x + g2 * rms_norm(f, ffn_post_g[l])
    return x


MIX_WIDTH = D_MODEL
MLA_WIDTH = MIX_WIDTH // 2
RET_WIDTH = MIX_WIDTH - MLA_WIDTH
MLA_HEADS = 4
MLA_NOPE_DIM = 128
MLA_ROPE_DIM = 64
MLA_QK_DIM = MLA_NOPE_DIM + MLA_ROPE_DIM
MLA_V_DIM = MLA_WIDTH // MLA_HEADS
MLA_Q_RANK = 256
MLA_KV_RANK = 128
Q_BLOCK = 128
RET_HEADS = 4
RET_HEAD_DIM = RET_WIDTH // RET_HEADS
RET_CHUNK = 128
MEM_TOKENS = 256
CROSS_HEADS = 4
CROSS_HEAD_DIM = D_MODEL // CROSS_HEADS
N_GROUPS = 4
EXPERTS_PER_GROUP = 8
N_EXPERTS = N_GROUPS * EXPERTS_PER_GROUP
TOP_K = 2
EXPERT_FF = 256
ROPE_BASE = 10000.0
NEG_INF = -1e30
IN_SPLITS = (MLA_Q_RANK, MLA_KV_RANK, MLA_ROPE_DIM, RET_WIDTH, RET_WIDTH, RET_WIDTH, RET_WIDTH)
IN_COLS = sum(IN_SPLITS)


def rms_norm_2(x, g):
    xf = x.astype(jnp.float32)
    y = xf * lax.rsqrt(jnp.mean(xf * xf, axis=-1, keepdims=True) + EPS)
    return (y * g.astype(jnp.float32)).astype(x.dtype)

def rope(x, positions):
    half = x.shape[-1] // 2
    inv_freq = ROPE_BASE ** (-jnp.arange(half, dtype=jnp.float32) / half)
    ang = positions.astype(jnp.float32)[:, :, None] * inv_freq
    cos = jnp.cos(ang)[:, :, None, :]
    sin = jnp.sin(ang)[:, :, None, :]
    xf = x.astype(jnp.float32)
    x1, x2 = xf[..., :half], xf[..., half:]
    return jnp.concatenate([x1 * cos - x2 * sin, x2 * cos + x1 * sin], axis=-1).astype(x.dtype)

def causal_block_attention(q, k, v):
    B, S, H, dq = q.shape
    dv = v.shape[-1]
    nb = S // Q_BLOCK
    scale = dq ** -0.5
    qb = q.reshape(B, nb, Q_BLOCK, H, dq).transpose(1, 0, 2, 3, 4)
    k_idx = jnp.arange(S)

    def one_block(args):
        q_blk, b = args
        s = jnp.einsum('bqhd,bkhd->bhqk', q_blk, k, preferred_element_type=jnp.float32) * scale
        q_idx = b * Q_BLOCK + jnp.arange(Q_BLOCK)
        s = jnp.where(k_idx[None, :] <= q_idx[:, None], s, NEG_INF)
        p = jax.nn.softmax(s, axis=-1).astype(v.dtype)
        return jnp.einsum('bhqk,bkhd->bqhd', p, v)

    out = lax.map(one_block, (qb, jnp.arange(nb)))
    return out.transpose(1, 0, 2, 3, 4).reshape(B, S, H, dv)

def retention_chunkwise(q, k, v):
    B, S, H, dk = q.shape
    dv = v.shape[-1]
    nc = S // RET_CHUNK

    def to_chunks(t):
        return t.astype(jnp.float32).reshape(B, nc, RET_CHUNK, H, t.shape[-1]).transpose(1, 0, 3, 2, 4)

    lg = jnp.log(1.0 - jnp.exp2(-5.0 - jnp.arange(H, dtype=jnp.float32)))
    idx = jnp.arange(RET_CHUNK, dtype=jnp.float32)
    diff = idx[:, None] - idx[None, :]
    intra = jnp.where(diff >= 0, jnp.exp(jnp.maximum(diff, 0.0)[None] * lg[:, None, None]), 0.0)
    q_decay = jnp.exp((idx + 1.0)[None] * lg[:, None])[:, :, None]
    k_decay = jnp.exp((RET_CHUNK - 1.0 - idx)[None] * lg[:, None])[:, :, None]
    chunk_decay = jnp.exp(RET_CHUNK * lg)[:, None, None]

    def step(state, qkv):
        qc, kc, vc = qkv
        scores = jnp.einsum('bhid,bhjd->bhij', qc, kc) * intra
        o = (jnp.einsum('bhij,bhjv->bhiv', scores, vc)
             + jnp.einsum('bhid,bhdv->bhiv', qc * q_decay, state))
        state = state * chunk_decay + jnp.einsum('bhjd,bhjv->bhdv', kc * k_decay, vc)
        return state, o

    state0 = jnp.zeros((B, H, dk, dv), jnp.float32)
    _, o = lax.scan(step, state0, (to_chunks(q), to_chunks(k), to_chunks(v)))
    return o.transpose(1, 0, 3, 2, 4).reshape(B, S, H, dv)

def mla_group(c_q, c_kv, k_pe, positions, q_norm_g, w_uq, kv_norm_g, w_ukv, q_qk_g, k_qk_g):
    B, S, _ = c_q.shape
    q = (rms_norm_2(c_q, q_norm_g) @ w_uq).reshape(B, S, MLA_HEADS, MLA_QK_DIM)
    kv = (rms_norm_2(c_kv, kv_norm_g) @ w_ukv).reshape(B, S, MLA_HEADS, MLA_NOPE_DIM + MLA_V_DIM)
    k_nope, v = kv[..., :MLA_NOPE_DIM], kv[..., MLA_NOPE_DIM:]
    k_rope = jnp.broadcast_to(k_pe[:, :, None, :], (B, S, MLA_HEADS, MLA_ROPE_DIM))
    k = jnp.concatenate([k_nope, k_rope], axis=-1)
    q = rms_norm_2(q, q_qk_g)
    k = rms_norm_2(k, k_qk_g)
    q = jnp.concatenate([q[..., :MLA_NOPE_DIM], rope(q[..., MLA_NOPE_DIM:], positions)], axis=-1)
    k = jnp.concatenate([k[..., :MLA_NOPE_DIM], rope(k[..., MLA_NOPE_DIM:], positions)], axis=-1)
    o = causal_block_attention(q, k, v)
    return o.reshape(B, S, MLA_WIDTH)

def retention_group(rq, rk, rv, rg, positions, gn_g):
    B, S, _ = rq.shape
    q = rope(rq.reshape(B, S, RET_HEADS, RET_HEAD_DIM), positions)
    k = rope(rk.reshape(B, S, RET_HEADS, RET_HEAD_DIM), positions) * (RET_HEAD_DIM ** -0.5)
    v = rv.reshape(B, S, RET_HEADS, RET_HEAD_DIM)
    o = retention_chunkwise(q, k, v)
    mu = jnp.mean(o, axis=-1, keepdims=True)
    var = jnp.mean(jnp.square(o - mu), axis=-1, keepdims=True)
    o = ((o - mu) * lax.rsqrt(var + EPS)).reshape(B, S, RET_WIDTH) * gn_g.astype(jnp.float32)
    return (o * jax.nn.silu(rg.astype(jnp.float32))).astype(rq.dtype)

def memory_cross_attention(h, m, w_q, w_kv, q_qk_g, k_qk_g, w_o):
    B, S, _ = h.shape
    M = m.shape[1]
    q = rms_norm_2((h @ w_q).reshape(B, S, CROSS_HEADS, CROSS_HEAD_DIM), q_qk_g)
    kv = m @ w_kv
    k = rms_norm_2(kv[..., :D_MODEL].reshape(B, M, CROSS_HEADS, CROSS_HEAD_DIM), k_qk_g)
    v = kv[..., D_MODEL:].reshape(B, M, CROSS_HEADS, CROSS_HEAD_DIM)
    s = jnp.einsum('bshd,bmhd->bhsm', q, k, preferred_element_type=jnp.float32) * (CROSS_HEAD_DIM ** -0.5)
    p = jax.nn.softmax(s, axis=-1).astype(v.dtype)
    o = jnp.einsum('bhsm,bmhd->bshd', p, v).reshape(B, S, D_MODEL)
    return o @ w_o

def hierarchical_moe(h, w_group, b_group, w_expert, b_expert, w_gate, w_up, w_down):
    def per_row(hr):
        S = hr.shape[0]
        g_logits = jnp.einsum('sd,dg->sg', hr, w_group, preferred_element_type=jnp.float32)
        g_prob = jax.nn.softmax(g_logits, axis=-1)
        g_sel = jnp.argmax(g_logits + b_group.astype(jnp.float32), axis=-1)
        g_w = jnp.take_along_axis(g_prob, g_sel[:, None], axis=-1)
        e_all = jnp.einsum('sd,de->se', hr, w_expert, preferred_element_type=jnp.float32)
        e_all = e_all.reshape(S, N_GROUPS, EXPERTS_PER_GROUP)
        e_logits = jnp.take_along_axis(e_all, g_sel[:, None, None], axis=1)[:, 0]
        e_bias = b_expert.astype(jnp.float32).reshape(N_GROUPS, EXPERTS_PER_GROUP)[g_sel]
        e_prob = jax.nn.softmax(e_logits, axis=-1)
        _, top_idx = lax.top_k(e_logits + e_bias, TOP_K)
        top_p = jnp.take_along_axis(e_prob, top_idx, axis=-1)
        top_p = top_p / jnp.sum(top_p, axis=-1, keepdims=True)
        local_w = jnp.sum(jax.nn.one_hot(top_idx, EXPERTS_PER_GROUP, dtype=jnp.float32) * top_p[..., None], axis=1)
        gate = (jax.nn.one_hot(g_sel, N_GROUPS, dtype=jnp.float32)[:, :, None]
                * local_w[:, None, :] * g_w[:, :, None]).reshape(S, N_EXPERTS)
        a = jnp.einsum('sd,edf->sef', hr, w_gate)
        u = jnp.einsum('sd,edf->sef', hr, w_up)
        act = jax.nn.silu(a) * u * gate[:, :, None].astype(hr.dtype)
        return jnp.einsum('sef,efd->sd', act, w_down)

    return lax.map(per_row, h)

def second_inputs(seed: int = 0) -> dict:
    key = jax.random.key(seed)
    ks = jax.random.split(key, 32)

    def w(k, shape, fan_in):
        return jax.random.normal(k, (DEPTH,) + shape, jnp.float32) * (fan_in ** -0.5)

    def gain(k, n):
        return 1.0 + 0.02 * jax.random.normal(k, (DEPTH, n), jnp.float32)

    def bias(k, n):
        return 0.01 * jax.random.normal(k, (DEPTH, n), jnp.float32)

    x = jax.random.normal(ks[0], (BATCH, SEQ, D_MODEL), jnp.float32)
    mem = jax.random.normal(ks[1], (BATCH, MEM_TOKENS, D_MODEL), jnp.float32)
    offsets = jax.random.randint(ks[2], (BATCH, 1), 0, 1024, dtype=jnp.int32)
    positions = offsets + jnp.arange(SEQ, dtype=jnp.int32)[None, :]
    return {
        'x': x,
        'mem': mem,
        'positions': positions,
        'attn_norm_g': gain(ks[3], D_MODEL),
        'w_in': w(ks[4], (D_MODEL, IN_COLS), D_MODEL),
        'mla_q_norm_g': gain(ks[5], MLA_Q_RANK),
        'mla_w_uq': w(ks[6], (MLA_Q_RANK, MLA_HEADS * MLA_QK_DIM), MLA_Q_RANK),
        'mla_kv_norm_g': gain(ks[7], MLA_KV_RANK),
        'mla_w_ukv': w(ks[8], (MLA_KV_RANK, MLA_HEADS * (MLA_NOPE_DIM + MLA_V_DIM)), MLA_KV_RANK),
        'mla_q_qk_g': gain(ks[9], MLA_QK_DIM),
        'mla_k_qk_g': gain(ks[10], MLA_QK_DIM),
        'ret_gn_g': gain(ks[11], RET_WIDTH),
        'w_out': w(ks[12], (MIX_WIDTH, D_MODEL), MIX_WIDTH),
        'cross_norm_g': gain(ks[13], D_MODEL),
        'mem_norm_g': gain(ks[14], D_MODEL),
        'cross_w_q': w(ks[15], (D_MODEL, D_MODEL), D_MODEL),
        'cross_w_kv': w(ks[16], (D_MODEL, 2 * D_MODEL), D_MODEL),
        'cross_q_qk_g': gain(ks[17], CROSS_HEAD_DIM),
        'cross_k_qk_g': gain(ks[18], CROSS_HEAD_DIM),
        'cross_w_o': w(ks[19], (D_MODEL, D_MODEL), D_MODEL),
        'moe_norm_g': gain(ks[20], D_MODEL),
        'router_w_group': w(ks[21], (D_MODEL, N_GROUPS), D_MODEL),
        'router_b_group': bias(ks[22], N_GROUPS),
        'router_w_expert': w(ks[23], (D_MODEL, N_EXPERTS), D_MODEL),
        'router_b_expert': bias(ks[24], N_EXPERTS),
        'expert_w_gate': w(ks[25], (N_EXPERTS, D_MODEL, EXPERT_FF), D_MODEL),
        'expert_w_up': w(ks[26], (N_EXPERTS, D_MODEL, EXPERT_FF), D_MODEL),
        'expert_w_down': w(ks[27], (N_EXPERTS, EXPERT_FF, D_MODEL), EXPERT_FF),
    }

def second_block(x, mem, positions, attn_norm_g, w_in, mla_q_norm_g, mla_w_uq, mla_kv_norm_g, mla_w_ukv,
              mla_q_qk_g, mla_k_qk_g, ret_gn_g, w_out, cross_norm_g, mem_norm_g, cross_w_q, cross_w_kv,
              cross_q_qk_g, cross_k_qk_g, cross_w_o, moe_norm_g, router_w_group, router_b_group,
              router_w_expert, router_b_expert, expert_w_gate, expert_w_up, expert_w_down):
    split_points = [int(s) for s in np.cumsum(IN_SPLITS)[:-1]]
    for l in range(DEPTH):
        h = rms_norm_2(x, attn_norm_g[l])
        proj = h @ w_in[l]
        c_q, c_kv, k_pe, rq, rk, rv, rg = jnp.split(proj, split_points, axis=-1)
        a_out = mla_group(c_q, c_kv, k_pe, positions, mla_q_norm_g[l], mla_w_uq[l],
                          mla_kv_norm_g[l], mla_w_ukv[l], mla_q_qk_g[l], mla_k_qk_g[l])
        r_out = retention_group(rq, rk, rv, rg, positions, ret_gn_g[l])
        x = x + jnp.concatenate([a_out, r_out], axis=-1) @ w_out[l]
        hc = rms_norm_2(x, cross_norm_g[l])
        m = rms_norm_2(mem, mem_norm_g[l])
        x = x + memory_cross_attention(hc, m, cross_w_q[l], cross_w_kv[l], cross_q_qk_g[l],
                                       cross_k_qk_g[l], cross_w_o[l])
        hm = rms_norm_2(x, moe_norm_g[l])
        x = x + hierarchical_moe(hm, router_w_group[l], router_b_group[l], router_w_expert[l],
                                 router_b_expert[l], expert_w_gate[l], expert_w_up[l], expert_w_down[l])
    return x


def setup_inputs(seed=0):
    out = dict(first_inputs(seed))
    for name, value in second_inputs(seed + 1).items():
        if name != "x":
            out[name + "_2"] = value
    return out


def reference(
    x, c, ada_w, ada_b, mix_pre_g, mix_post_g, w_in, qk_conv_w, qk_conv_b, igate_b, fgate_b,
    ml_norm_g, cv_dw_w, cv_dw_b, cv_ln_g, cv_ln_b, w_out, ffn_pre_g, ffn_post_g, ffn_up,
    ffn_conv_w, ffn_conv_b, ffn_down, mem_2, positions_2, attn_norm_g_2, w_in_2, mla_q_norm_g_2,
    mla_w_uq_2, mla_kv_norm_g_2, mla_w_ukv_2, mla_q_qk_g_2, mla_k_qk_g_2, ret_gn_g_2, w_out_2,
    cross_norm_g_2, mem_norm_g_2, cross_w_q_2, cross_w_kv_2, cross_q_qk_g_2, cross_k_qk_g_2,
    cross_w_o_2, moe_norm_g_2, router_w_group_2, router_b_group_2, router_w_expert_2,
    router_b_expert_2, expert_w_gate_2, expert_w_up_2, expert_w_down_2,
):
    x = first_block(
        x, c, ada_w, ada_b, mix_pre_g, mix_post_g, w_in, qk_conv_w, qk_conv_b, igate_b, fgate_b,
        ml_norm_g, cv_dw_w, cv_dw_b, cv_ln_g, cv_ln_b, w_out, ffn_pre_g, ffn_post_g, ffn_up,
        ffn_conv_w, ffn_conv_b, ffn_down,
    )
    return second_block(
        x, mem_2, positions_2, attn_norm_g_2, w_in_2, mla_q_norm_g_2, mla_w_uq_2,
        mla_kv_norm_g_2, mla_w_ukv_2, mla_q_qk_g_2, mla_k_qk_g_2, ret_gn_g_2, w_out_2,
        cross_norm_g_2, mem_norm_g_2, cross_w_q_2, cross_w_kv_2, cross_q_qk_g_2, cross_k_qk_g_2,
        cross_w_o_2, moe_norm_g_2, router_w_group_2, router_b_group_2, router_w_expert_2,
        router_b_expert_2, expert_w_gate_2, expert_w_up_2, expert_w_down_2,
    )


_drawn_inputs = setup_inputs


def setup_inputs(seed=0):
    import zlib

    import numpy as np

    out = dict(_drawn_inputs(seed))
    spreads = {}
    factors = {'qk_conv_b': 8.0,
     'igate_b': 64.0,
     'cv_ln_b': 4.01,
     'ffn_conv_b': 2.695,
     'mla_q_norm_g_2': 8.0,
     'mla_kv_norm_g_2': 4.907,
     'mla_q_qk_g_2': 8.0,
     'mla_k_qk_g_2': 8.0,
     'ret_gn_g_2': 2.835,
     'cross_norm_g_2': 8.0,
     'mem_norm_g_2': 6.04,
     'cross_q_qk_g_2': 7.22,
     'cross_k_qk_g_2': 8.0,
     'router_b_expert_2': 64.0,
     'moe_norm_g_2': 8.0}
    for name, (base, spread) in spreads.items():
        noise = np.random.default_rng([zlib.crc32(name.encode()), seed]).standard_normal(out[name].shape)
        drawn = base * np.exp(spread * noise) if base else spread * noise
        out[name] = __import__('jax').numpy.asarray(drawn.astype(out[name].dtype))
    for name, factor in factors.items():
        out[name] = (out[name] * factor).astype(out[name].dtype)
    return out
```

```python
from contextlib import ExitStack

import numpy as np
import concourse.bass as bass
from concourse import mybir

ALU = mybir.AluOpType
ACT = mybir.ActivationFunctionType
F32 = mybir.dt.float32
F32R = mybir.dt.float32r
I32 = mybir.dt.int32
U32 = mybir.dt.uint32
AX = mybir.AxisListType.X

P = 128
T = 512
NT = T // P
D = 1024
ND = D // P
NH = 4
HD = 256
CV = 31
QC = 4
FC = 3
DFF = 2816
NF = DFF // P
MEM = 256
NM = MEM // P
NOPE, ROPE = 128, 64
QKD = NOPE + ROPE
NE, NG, EG = 32, 4, 8
EF = 256
NB = NE + 2 * T // P
NBX = NB + 4
EPS = 1e-6
NEG = -1e30
SLOTS = 4
CW = 1480
PANEL = 2048

VECTORS = [
    ("c", 8), ("ada_b", 48), ("mix_pre_g", 8), ("mix_post_g", 8), ("qk_conv_w", 64), ("qk_conv_b", 16),
    ("ml_norm_g", 8), ("cv_dw_w", 248), ("cv_dw_b", 8), ("cv_ln_g", 8), ("cv_ln_b", 8),
    ("ffn_pre_g", 8), ("ffn_post_g", 8), ("ffn_conv_w", 132), ("ffn_conv_b", 44),
    ("attn_norm_g_2", 8), ("mla_q_norm_g_2", 2), ("mla_kv_norm_g_2", 1), ("mla_q_qk_g_2", 2), ("mla_k_qk_g_2", 2),
    ("ret_gn_g_2", 4), ("cross_norm_g_2", 8), ("mem_norm_g_2", 8), ("cross_q_qk_g_2", 2), ("cross_k_qk_g_2", 2),
    ("moe_norm_g_2", 8),
]
COL = {}
_n = 0
for _name, _rows in VECTORS:
    COL[_name] = _n
    _n += _rows
NV = _n
VG = -(-NV // P)


def constants():
    i = np.arange(P, dtype=np.float32)
    c = np.zeros((P, CW + 2048), np.float32)
    c[:, 0:128] = np.eye(P)
    c[:, 128:256] = 1.0
    c[:, 256:384] = (i[None, :] >= i[:, None])
    c[:, 384:512] = np.where(i[None, :] > i[:, None], NEG, 0.0)
    c[:, 512:640] = (i[:, None] < i[None, :])
    for h in range(NH):
        c[h, 640 + 128 * h:768 + 128 * h] = 1.0
    for m in range(P):
        if m < 64:
            c[m + 64, 1152 + m] = -1.0
        else:
            c[m - 64, 1152 + m] = 1.0
    for m in range(64):
        if m < 32:
            c[m + 32, 1280 + m] = -1.0
        else:
            c[m - 32, 1280 + m] = 1.0
    c[:, 1344] = np.float32(10000.0) ** (-(np.arange(P) % 64).astype(np.float32) / np.float32(64))
    c[:, 1345] = np.float32(10000.0) ** (-(np.arange(P) % 32).astype(np.float32) / np.float32(32))
    c[:, 1346] = EPS
    for t in range(NT):
        c[:, 1348 + t] = i + 128 * t
    c[:, 1352:1480] = i[None, :]
    lg = np.log(1.0 - np.exp2(-5.0 - np.arange(NH, dtype=np.float64)))
    t = np.arange(T)[None, :] - np.arange(P)[:, None]
    for h in range(NH):
        c[:, CW + 512 * h:CW + 512 * h + 512] = np.where(t >= 0, np.exp(np.maximum(t, 0) * lg[h]), 0.0) * 128.0 ** -0.5
    return c


class Job:

    def __init__(self, bank, nth):
        self.bank, self.nth = bank, nth


def plan_jobs():
    order = [("vec", 2), ("xT", 8), ("n1s", 1), ("modA", 1), ("n1r", 1), ("glu", 16), ("gates", 2), ("qk", 16), ("v", 8),
             ("gT", 1), ("o", 8), ("Mb0", 1), ("S0", 4)]
    for h in range(1, NH):
        order += [(f"Mb{h}", 1), (f"S{h}", 4), (f"N{h - 1}", 4)]
        if h > 1:
            order += [(("lms", "lmr")[h - 2], 1)]
    order += [(f"N{NH - 1}", 4), ("lvs", 1), ("lvr", 1), ("wo", 8), ("n2s", 1), ("modB", 1), ("n2r", 1),
              ("n3s", 1), ("n3r", 1), ("up", 44), ("down", 8), ("n4s", 1), ("n4r", 1)]
    order += [("n5s", 1), ("n5r", 1), ("cq", 2), ("ckv", 1), ("kpe", 1), ("cqs", 1), ("cqr", 1), ("cks", 1), ("ckr", 1),
              ("qn", 4), ("qr", 4), ("kn", 4), ("mv", 4), ("krot", 1), ("qrot", 4), ("qs", 1), ("ks", 1), ("qR", 4), ("kR", 4)]
    for h in range(NH + 1):
        order += [(f"A{h}", 4)] * (h < NH) + [(f"AT{h - 1}", 4), (f"AO{h - 1}", 1)] * (h > 0)
    order += [("rqk", 8), ("rrot", 8), ("rv", 4), ("rg", 4)]
    for h in range(NH + 1):
        order += [(f"R{h}", 4)] * (h < NH) + [(f"RO{h - 1}", 1)] * (h > 0)
    order += [("gms", 1), ("gmr", 4), ("gvs", 1), ("gvr", 4), ("wo2", 8)]
    order += [("n6s", 1), ("n6r", 1), ("memT", 4), ("nms", 1), ("nmr", 1), ("xq", 8), ("xk", 8), ("xv", 4),
              ("xqs", 1), ("xqr", 4), ("xks", 1), ("xkr", 4)]
    for h in range(NH + 1):
        order += [(f"X{h}", 4)] * (h < NH) + [(f"XT{h - 1}", 2), (f"XO{h - 1}", 2)] * (h > 0)
    order += [("xo", 8), ("n7s", 1), ("n7r", 1), ("bias", 1), ("logit", 1), ("hmT", 8), ("xTM", 8), ("rank", 1), ("tab", 1)]
    jobs, n, filled = {}, 0, [0] * 8

    def fill(b):
        filled[b % 8] += 1
        return Job(b % 8, filled[b % 8])

    for name, count in order:
        if name == "wo":
            jobs["wo"] = [fill(n + i) for i in range(4)]
            jobs["hT"] = [fill(n + 4 + i % 4) for i in range(8)]
            jobs["wo"] += [fill(n + 4 + i) for i in range(4)]
            continue
        jobs[name] = [fill(n + i) for i in range(count)]
        n += count
    return jobs


NORM_LIST = [
    ("n1", [8], NT, D, "rms"), ("lm", [8], NT, D, "mean"), ("lv", [8], NT, D, "rms"), ("n2", [8], NT, D, "rms"),
    ("n3", [8], NT, D, "rms"), ("n4", [8], NT, D, "rms"), ("n5", [8], NT, D, "rms"), ("cq", [2], NT, 256, "rms"),
    ("ck", [1], NT, 128, "rms"), ("q", [2] * 4, NT, QKD, "rms"), ("k", [2] * 4, NT, QKD, "rms"),
    ("gm", [1] * 4, NT, 128, "mean"), ("gv", [1] * 4, NT, 128, "rms"), ("n6", [8], NT, D, "rms"), ("nm", [8], NM, D, "rms"),
    ("xq", [2] * 4, NT, HD, "rms"), ("xk", [2] * 4, NM, HD, "rms"), ("n7", [8], NT, D, "rms"),
]
NORMS = {n[0]: n[1:] for n in NORM_LIST}
RJOB = {n: n + "r" for n in NORMS}
RJOB.update(q="qR", k="kR")
SQUARES = [("n1", 8), ("lv", 8), ("n2", 8), ("n3", 8), ("n4", 8), ("n5", 8), ("cq", 2), ("ck", 1), ("kpe", 1), ("q", 8), ("k", 4),
           ("gv", 4), ("n6", 8), ("nm", 8), ("xq", 8), ("xk", 8), ("n7", 8)]
SQ = {}
_n = 0
for _name, _c in SQUARES:
    SQ[_name] = (_n, _n + _c)
    _n += _c
DIAG = {}
DIAG_JOBS = []
for _name, _sizes, *_ in NORM_LIST:
    DIAG[_name] = len(DIAG_JOBS)
    DIAG_JOBS += [(RJOB[_name], _g) for _g in range(len(_sizes))]
SCALED = {}
_n = 0
for _name, _c in (("n1", 7), ("lv", 7), ("n3", 7), ("n5", 7), ("cq", 1), ("ck", 0), ("n6", 7), ("nm", 7), ("n7", 7)):
    SCALED[_name] = _n
    _n += _c
SHIFTED = {"n1": 0, "n3": 8}
FROM_X = {"n1", "n3", "n5", "n6", "n7"}
NOPE_GAIN, ROPE_GAIN, XQ_GAIN = 32, 33, 34
GA_EM, GD_M = 4, 7
RD_R = 5


DOWN_PARTS = [(0, 8), (8, 15), (15, 22)]


def rep(eng, n):
    with eng.Fori(0, n) as i:
        yield i


def plan_panels(w):
    ada, w_in, w_out, up, down = w["ada_w"], w["w_in"], w["w_out"], w["ffn_up"], w["ffn_down"]
    out = []

    def cols(src, lo, width, job):
        out.append((src[:, lo:lo + width], job, False))

    def split(src, lo, job):
        out.append((src[:, lo:lo + P], job, True))

    for p in range(8):
        cols(ada, 256 * p, 256, ("mod", p))
    for p in range(4):
        cols(w_in, 4104 + 256 * p, 256, ("glu", 4 * p + 1))
        cols(w_in, 5128 + 256 * p, 256, ("glu", 4 * p + 3))
    for p in range(8):
        cols(w_in, 256 * p, 256, ("qk", 2 * p + 1))
    for p in range(4):
        cols(w_in, 2048 + 256 * p, 256, ("v", 2 * p + 1))
    for p in range(4):
        cols(w_in, 3072 + 256 * p, 256, ("o", 2 * p + 1))
    for p in range(8):
        cols(w_out, 128 * p, 128, ("wo", p))
        if p >= 4:
            for q in range(4 * p - 8, 4 * p - 4):
                cols(ada, 256 * q, 256, ("mod", q))
    for p in range(11):
        for j in range(2):
            for half in range(2):
                split(up, DFF * j + P * (2 * p + half), ("up", 4 * p + 2 * j + half))
    for p in range(8):
        for i, (lo, hi) in enumerate(DOWN_PARTS):
            split(down[P * lo:P * hi], P * p, ("part", 2 * p + i) if i < 2 else ("down", p))
    w2 = w["w_in_2"]
    cols(w2, 0, 256, ("cq", 1))
    cols(w2, 256, 192, ("kpe", 0))
    out.append((w["mla_w_uq_2"], ("qr", 3), False))
    out.append((w["mla_w_ukv_2"], ("mv", 3), False))
    for p in range(4):
        cols(w2, 448 + 256 * p, 256, ("rqk", 2 * p + 1))
    for p in range(2):
        cols(w2, 1472 + 256 * p, 256, ("rv", 2 * p + 1))
    for p in range(2):
        cols(w2, 1984 + 256 * p, 256, ("rg", 2 * p + 1))
    for p in range(4):
        cols(w["w_out_2"], 256 * p, 256, ("wo2", 2 * p + 1))
    for p in range(4):
        cols(w["cross_w_q_2"], 256 * p, 256, ("xq", 2 * p + 1))
    for p in range(4):
        cols(w["cross_w_kv_2"], 256 * p, 256, ("xk", 2 * p + 1))
    for p in range(4):
        cols(w["cross_w_kv_2"], 1024 + 256 * p, 256, ("xv", p))
    for p in range(4):
        cols(w["cross_w_o_2"], 256 * p, 256, ("xo", 2 * p + 1))
    return out


def program(nc, w, out):
    jobs = plan_jobs()
    panels = plan_panels(w)
    split_panels = [n for n, (_, _, split) in enumerate(panels) if split]
    mod_panels = [n for n, (_, reader, _) in enumerate(panels) if reader[0] == "mod"]
    with ExitStack() as ctx:
        def sb(name, width, dt=F32, rows=P):
            return ctx.enter_context(nc.sbuf_tensor(name, [rows, width], dt))[:, :]

        def sem(name):
            return ctx.enter_context(nc.semaphore(name))

        with nc.sbuf_tensor("ring", [P, SLOTS * PANEL], F32) as t0, nc.sbuf_tensor("uT", [P, ND * T], F32) as t1, \
                nc.sbuf_tensor("sq", [P, ND * T], F32) as t2, nc.sbuf_tensor("arena", [P, 24832], F32) as t3:
            ring, uf, sqf, arena = t0[:, :], t1[:, :], t2[:, :], t3[:, :]
        ring_parts, u_low, u_high, arena_parts = (sb("ring_parts", SLOTS * PANEL, F32R), sb("u_low", ND * T, F32R), sb("u_high", ND * T, F32R),
                                                  sb("arena_parts", 24832, F32R))
        uL, uH = u_low.rearrange("p (k t) -> p k t", k=ND), u_high.rearrange("p (k t) -> p k t", k=ND)
        fL, fH = (arena_parts[:, NF * T * i:NF * T * (i + 1)].rearrange("p (k t) -> p k t", k=NF) for i in range(2))
        xT = sb("xT", ND * T).rearrange("p (k t) -> p k t", k=ND)
        uT = uf.rearrange("p (k t) -> p k t", k=ND)
        sq = sqf.rearrange("p (k t) -> p k t", k=ND)
        const = sb("const", CW)
        vec = sb("vec", NV)
        mod = sb("mod", 48)
        gain = sb("gain", 48)
        cond = sb("cond", 8)
        stat = sb("stat", 4 * 16).rearrange("p (b c) -> p b c", b=4)
        soft = sb("soft", 3 * 32).rearrange("p (b c) -> p b c", b=3)
        dg = sb("dg", 2 * T).rearrange("p (b t) -> p b t", b=2)
        tA = sb("tA", 4 * T).rearrange("p (b t) -> p b t", b=4)
        tB = sb("tB", 2 * T).rearrange("p (b t) -> p b t", b=2)
        wg = sb("wg", 8 * 8)
        small = sb("small", 240)

        def view(lo, k, width):
            return arena[:, lo:lo + k * width].rearrange("p (k t) -> p k t", k=k)

        ident, ones, tri, neg, below = (const[:, 128 * i:128 * i + 128] for i in range(5))
        sel = [const[0:4, 640 + 128 * h:768 + 128 * h] for h in range(NH)]
        rot128, rot64 = const[:, 1152:1280], const[0:64, 1280:1344]
        eps = const[:, 1346:1347]
        vrows = tA[:, :, :].rearrange("p b t -> p (b t)")[:, 0:VG * P].rearrange("p (g c) -> p g c", g=VG)
        xTM = view(12304, NT, D)
        qk = view(0, 16, T)
        v1 = arena[:, 8192:12304].rearrange("p (t h e) -> p t h e", t=NT, h=NH)
        og = view(12304, NT, D)
        ypad = view(16400, 8, T + CV - 1)
        hn = view(16400, NT, D)
        yc = view(20736, 8, T)
        hT = view(0, 8, T)
        accA, accB = view(20736, 8, 256), view(16400, 16, 256)
        prob = [sqf[:, 2048 * b:2048 * b + 2048].rearrange("p (s t) -> p s t", s=NT) for b in range(2)]
        rows = {nm: arena[0:4, 12304 + T * i:12304 + T * i + T] for i, nm in enumerate(("i", "f", "e", "B", "a", "m", "em", "one"))}
        Mrow = dg[0:4, 0, :]
        aT, emT = small[:, 0:16], small[:, 16:32]
        den, ssq, fin = small[:, 32:48], small[:, 48:64], small[:, 64:80]
        t16 = small[:, 80:96]
        fT = view(0, NF, T)
        cq, ckv, kpe = view(0, 2, T), arena[:, 1024:1536], arena[0:64, 1536:2048]
        trig = view(22528, 4, T)
        qn, kn = view(4096, NH, T), view(8192, NH, T)
        qr = arena[0:64, 6144:8192].rearrange("p (h t) -> p h t", h=NH)
        kr = arena[0:64, 10240:12288].rearrange("p (h t) -> p h t", h=NH)
        mv = view(12288, NT, NH * P)
        att = prob
        attT = [view(14336 + 2048 * b, NT, T) for b in range(2)]
        cat = view(18432, 8, T)
        rqk = view(4096, 8, T)
        rv, rg = view(8192, NT, T), view(10240, NH, T)
        decay = view(12288, NH, T)
        memTM = view(2048, NM, D)
        xq, xk, xv = view(0, 8, T), view(4096, 8, MEM), view(6144, NM, D)
        memT = view(10240, 8, MEM)
        xp = [view(12288 + 1024 * b, NT, MEM) for b in range(2)]
        xpT = [view(14336 + 1024 * b, NM, T) for b in range(2)]
        xoT = view(16384, 8, T)
        posI = arena[:, 12288:12800].bitcast(I32)
        qsq = lambda g, k: sq[0:(P, ROPE)[k], 4 * k + g, :]
        ksq = lambda g, k: cat[0:(P, ROPE)[k], 4 if k else g, :]
        xksq = view(12288, 8, MEM)
        wgu = [view(6144 * s, 8, 512) for s in range(SLOTS)]
        wdn = [view(6144 * s + 4096, 2, D) for s in range(SLOTS)]
        hmTM = ring[:, 0:4096].rearrange("p (k t) -> p k t", k=NT)
        xoutTM = ring[:, 4096:8192].rearrange("p (k t) -> p k t", k=NT)
        yb = [ring[:, 1024 * b:1024 * b + 1024] for b in range(4)]
        xg = [sqf[:, 1024 * b:1024 * b + 1024] for b in range(2)]
        xgT = [sqf[:, 2048 + 1024 * b:3072 + 1024 * b].rearrange("p (k t) -> p k t", k=8) for b in range(2)]
        pick = [uT[:, 2 * b:2 * b + 2, :].rearrange("p k t -> p (k t)") for b in range(4)]
        act_f = [tA[:, b, 0:256] for b in range(2)]
        act_m = [tA[:, b, 256:512] for b in range(2)]
        actT = [tB[:, b, 0:256].rearrange("p (j t) -> p j t", j=2) for b in range(2)]
        wr = view(20480, 8, 36)
        bias_row = arena[0:1, 20768:20804]

        def scratch(lo, *shape):
            n = int(np.prod(shape))
            names = " ".join("abcd"[:len(shape)])
            return arena[:, lo:lo + n].rearrange(f"p ({names}) -> p {names}", **dict(zip("abcd", shape)))

        r_L, r_Lb = scratch(0, NT, 36), scratch(200, 36)
        r_M, r_E = scratch(300, NT, NE), [scratch(500 + 128 * c, NT, NG, EG) for c in range(2)]
        r_A, r_B = scratch(1000, 8, P), scratch(2100, 8, NBX)
        expert_of = small[0:1, 96:96 + NBX].bitcast(I32)
        token_of = small[:, 140:140 + NBX].bitcast(I32)
        zeros = arena[:, 24576:24832]
        row_of = small[:, 184:192].bitcast(I32)
        share = small[:, 192:200]
        turn_count = small[0:1, 204:205].bitcast(I32)
        index = [small[:, 206 + b:207 + b].bitcast(I32) for b in range(2)]
        r_im, r_x, r_y = scratch(2600, 64), scratch(2680, NT, NG), scratch(2700, NT, EG)

        def cv(name, i=0, p=P):
            return vec[0:p, COL[name] + i:COL[name] + i + 1]

        hm_dram = nc.dram_tensor("hm_rows", [T, D], F32, kind="Internal").ap()
        y_dram = nc.dram_tensor("expert_rows", [NB * P, D], F32, kind="Internal").ap()

        bank = [ctx.enter_context(nc.psum_tensor(f"bank{b}", [P, 512], F32))[:, :] for b in range(8)]
        bank_full = [sem(f"bank_full{b}") for b in range(8)]
        bank_free = [sem(f"bank_free{b}") for b in range(8)]
        S = {}

        def named(*names):
            for nm in names:
                S[nm] = sem(nm)

        named("const_in", "x_in", "vec_zero", "vec_in", "wg_in", "mem_in", "pos_in", "decay_in", "rt_in",
              "cond_done", "mod_done", "mod_acc", "mod_chain", "gain_done", "sq_done", "diag_done", "scaled", "shifted", "glu_sig", "pad_zero",
              "conv_acc", "conv_done", "qk_affine", "qk_conv", "qk_done", "vone_done", "gate_act", "gate_dve",
              "w_sub", "w_exp", "w_mask", "h_sq", "h_chain", "h_done", "lv_sub", "lv_done", "x_upd",
              "up_affine", "up_conv", "up_silu", "f_done", "dve_chain", "act_chain", "rope_done",
              "att_max", "att_exp", "att_norm", "ret_sub", "rg_silu", "trig_act", "trig_dve",
              "route_dve", "route_act", "idx_done", "hm_out", "g_silu", "act_done", "moe_ok",
              "table_ready", "gather_go", "index_done", "out_sum", "out_done", "zeros_made", "y_zeroed", "panel_split", "panel_high", "part_read", "u_split", "f_high", "f_split")
        ring_full = [sem(f"ring_full{s}") for s in range(SLOTS)]
        moe_w = [sem(f"moe_weights{s}") for s in range(SLOTS)]
        moe_full = [sem(f"moe_full{b}") for b in range(7)]
        moe_free = [sem(f"moe_free{b}") for b in range(7)]
        gathered = [sem(f"gathered{b}") for b in range(2)]
        picked = [sem(f"picked{b}") for b in range(4)]
        y_out = [sem(f"rows_out{s}") for s in range(2)]

        def opened(job):
            nc.tensor.wait_ge(bank_free[job.bank], job.nth)

        def full(ins, job):
            ins.then_inc(bank_full[job.bank], 1)

        def see(eng, job):
            eng.wait_ge(bank_full[job.bank], job.nth)
            return bank[job.bank]

        def free(ins, job):
            ins.then_inc(bank_free[job.bank], 1)

        def freed(eng, job):
            eng.wait_ge(bank_free[job.bank], job.nth + 1)

        def J(name, i=0):
            return jobs[name][i]

        last = {}
        for group in (g for name, g in jobs.items() if name not in ("rank", "tab")):
            for job in group:
                if job.nth >= last.get(job.bank, job).nth:
                    last[job.bank] = job
        LAST = list(last.values())
        vector_rows = []
        for name, count in VECTORS:
            flat = w[name].flatten()
            if flat.shape[0] == QKD:
                vector_rows += [(COL[name], flat[0:NOPE].unsqueeze(0)), (COL[name] + 1, flat[NOPE:QKD].unsqueeze(0))]
                continue
            src, r = flat.rearrange("(r c) -> r c", c=P), 0
            while r < count:
                n = min(count - r, P - (COL[name] + r) % P)
                vector_rows.append((COL[name] + r, src[r:r + n, :]))
                r += n

        def panel_parts(n):
            base, size = PANEL * (n % SLOTS), panels[n][0].shape[0]
            return (ring[:, base:base + size], ring_parts[:, base + PANEL // 2:base + PANEL // 2 + size], ring_parts[:, base:base + size])

        def turns_of(eng):
            eng.wait_ge(S["table_ready"], 1)
            return eng.value_load(turn_count, min_val=2 * T // P // SLOTS, max_val=NB // SLOTS)

        block = ctx.enter_context(nc.Block())

        mark = {}

        @block.vector
        def _(dve):
            TS, TT, STT = dve.tensor_scalar, dve.tensor_tensor, dve.scalar_tensor_tensor
            chained = [0]

            def link(ins):
                chained[0] += 1
                ins.then_inc(S["dve_chain"], 1)
                dve.wait_ge(S["dve_chain"], chained[0])

            def count(name, ins):
                ins.then_inc(S[name], 1)

            def diagonals(name):
                sizes, nt, _, kind = NORMS[name]
                n, par = len(sizes) * nt, list(NORMS).index(name) % 2
                freed(dve, J(name + "s"))
                src = stat[:, par, 0:n]
                if kind == "rms":
                    link(dve.reciprocal(stat[:, 2 + par, 0:n], src))
                    src = stat[:, 2 + par, 0:n]
                for g in range(len(sizes)):
                    i = DIAG[name] + g
                    if i >= 2:
                        old, og_ = DIAG_JOBS[i - 2]
                        see(dve, J(old, og_))
                    count("diag_done", TT(dg[:, i % 2, 0:nt * P].rearrange("p (t c) -> p t c", t=nt), ident.unsqueeze(1).to_broadcast([P, nt, P]),
                                          src[:, g * nt:(g + 1) * nt].unsqueeze(2).to_broadcast([P, nt, P]), ALU.mult))

            def scale_tiles(name, dst, gain_of, n=ND, width=T):
                job = J(RJOB[name])
                b = see(dve, job)
                for k in range(n):
                    ins = STT(dst[:, k, :], dst[:, k, :] if name not in FROM_X else xT[:, k, :], gain_of(k), b[:, 0:width], ALU.mult, ALU.mult)
                    count("scaled", ins) if k < n - 1 else free(ins, job)

            def residual(name, gcol):
                job = J(RJOB[name])
                b = see(dve, job)
                for k in range(ND):
                    ins = STT(uT[:, k, :], uT[:, k, :], gain[:, gcol + k:gcol + k + 1], b, ALU.mult, ALU.mult)
                    if k < ND - 1:
                        link(ins)
                    else:
                        free(ins, job)
                        freed(dve, job)
                    count("x_upd", TT(xT[:, k, :], xT[:, k, :], uT[:, k, :], ALU.add))

            count("vec_zero", dve.memset(vrows, 0.0))
            link(dve.memset(ypad[:, :, 0:CV - 1], 0.0))
            for j in range(2):
                b = see(dve, J("vec", j))
                lo, hi = 512 * j, min(NV, 512 * j + 512)
                free(dve.tensor_copy(vec[:, lo:hi], b[:, 0:hi - lo]), J("vec", j))
            for k in range(ND):
                free(dve.tensor_copy(xT[:, k, :], see(dve, J("xT", k))), J("xT", k))
            freed(dve, J("vec", 0))
            freed(dve, J("vec", 1))
            def mod_sums(acc, first):
                for q0 in range(0, acc.shape[1], 2):
                    for k in range(ND):
                        for q in (q0, q0 + 1):
                            i = first + q
                            n = mod_panels[i]
                            if k == 0:
                                dve.wait_ge(ring_full[n % SLOTS], 16 * (n // SLOTS + 1))
                            else:
                                dve.wait_ge(S["mod_chain"], (ND - 1) * (first + q0) + 2 * (k - 1) + q - q0 + 1)
                            src = ring[:, PANEL * (n % SLOTS) + 256 * k:PANEL * (n % SLOTS) + 256 * k + 256]
                            if k == 0:
                                ins = TS(acc[:, q, :], src, cond[:, 0:1], None, ALU.mult)
                            else:
                                ins = STT(acc[:, q, :], src, cond[:, k:k + 1], acc[:, q, :], ALU.mult, ALU.add)
                            count("mod_acc" if k == ND - 1 else "mod_chain", ins)

            dve.wait_ge(S["cond_done"], 1)
            mod_sums(accA, 0)
            b = see(dve, J("modA"))
            free(TT(mod[:, 0:16], b[:, 0:16], vec[:, COL["ada_b"]:COL["ada_b"] + 16], ALU.add), J("modA"))
            freed(dve, J("modA"))
            dve.sem_inc(S["mod_done"], 1)
            vcols = lambda nm, n: vec[:, COL[nm]:COL[nm] + n]
            link(STT(gain[:, 0:8], mod[:, 8:16], 1.0, vcols("mix_pre_g", 8), ALU.add, ALU.mult))
            link(TS(gain[:, 32:34], vcols("mla_q_qk_g_2", 2), QKD ** -0.5, None, ALU.mult))
            link(TS(gain[:, 34:36], vcols("cross_q_qk_g_2", 2), HD ** -0.5, None, ALU.mult))
            diagonals("n1")
            for k in range(ND):
                freed(dve, J("xT", k))
            scale_tiles("n1", uT, lambda k: gain[:, k:k + 1])
            for p in range(4):
                for half in range(2):
                    a, g = J("glu", 4 * p + half), J("glu", 4 * p + 2 + half)
                    freed(dve, g)
                    free(TT(ypad[:, 2 * p + half, CV - 1:], see(dve, a), tB[:, half, :], ALU.mult), a)
            freed(dve, J("gates", 0))
            freed(dve, J("gates", 1))
            gsteps = [0]

            def gstep(ins):
                gsteps[0] += 1
                ins.then_inc(S["gate_dve"], 1)
                dve.wait_ge(S["gate_dve"], gsteps[0])

            gstep(dve.memset(rows["one"], 1.0))
            gstep(TS(rows["m"], rows["f"], 0.0, None, ALU.min))
            dve.wait_ge(S["gate_act"], 3)
            gstep(TT(rows["m"], rows["m"], rows["e"], ALU.subtract))
            gstep(dve.tensor_tensor_scan(rows["B"], rows["one"], rows["m"], 0.0, ALU.mult, ALU.add))
            gstep(TT(rows["a"], rows["i"], rows["B"], ALU.subtract))
            gstep(dve.tensor_tensor_scan(Mrow, rows["one"], rows["a"], 0.0, ALU.mult, ALU.max))
            gstep(TT(rows["m"], rows["B"], Mrow, ALU.add))
            assert gsteps[0] == GD_M

            def long_conv():
                for pair in range(4):
                    for tap in range(CV):
                        for q in range(2):
                            c = 2 * pair + q
                            if tap:
                                dve.wait_ge(S["conv_acc"], 2 * (CV - 1) * pair + 2 * (tap - 1) + q + 1)
                            src, wt = ypad[:, c, tap:tap + T], cv("cv_dw_w", 8 * tap + c)
                            if tap == 0:
                                ins = TS(yc[:, c, :], src, wt, cv("cv_dw_b", c), ALU.mult, ALU.add)
                            else:
                                ins = STT(yc[:, c, :], src, wt, yc[:, c, :], ALU.mult, ALU.add)
                            count("conv_done" if tap == CV - 1 else "conv_acc", ins)
                            yield

            conv = long_conv()

            def taps(n):
                for _ in range(n):
                    next(conv, None)

            for p in range(8):
                freed(dve, J("glu", 4 * (p // 2) + p % 2))
            steps = [0]

            def short_conv(ins, last=None):
                steps[0] += 1
                ins.then_inc(S["qk_conv"], 1)
                dve.wait_ge(S["qk_conv"], steps[0])

            for j in range(16):
                b = see(dve, J("qk", j))
                dve.wait_ge(S["qk_affine"], j + 1)
                for d in range(1, QC):
                    ins = STT(qk[:, j, d:T], b[:, 0:T - d], cv("qk_conv_w", 16 * (QC - 1 - d) + j), qk[:, j, d:T], ALU.mult, ALU.add)
                    short_conv(ins) if d < QC - 1 else free(ins, J("qk", j))
                    taps(1)
                taps(5)
            taps(62)
            free(dve.tensor_copy(small[:, 0:32], see(dve, J("gT"))[:, 0:32]), J("gT"))
            taps(62)
            freed(dve, J("gT"))

            def mweights(h):
                b = see(dve, J(f"Mb{h}"))
                for s in range(NT):
                    if h:
                        freed(dve, J(f"S{h - 1}", s))
                    ins = TS(tA[:, s, 0:T - P * s], b[:, P * s:T], aT[:, 4 * s + h:4 * s + h + 1], 0.0, ALU.subtract, ALU.max)
                    count("w_sub", ins) if s < NT - 1 else free(ins, J(f"Mb{h}"))

            def mscores(h):
                if h >= 2:
                    see(dve, J(f"N{h - 2}", 3))
                for s in range(NT):
                    b = see(dve, J(f"S{h}", s))
                    dve.wait_ge(S["w_mask"], NT * h + s + 1)
                    free(STT(prob[h % 2][:, s, 0:T - P * s], b[:, 0:T - P * s], HD ** -0.5, tA[:, s, 0:T - P * s], ALU.mult, ALU.mult), J(f"S{h}", s))

            def mnumer(h):
                for t in range(NT):
                    b = see(dve, J(f"N{h}", t))
                    link(dve.tensor_copy(hn[:, t, HD * h:HD * h + HD], b[:, 0:HD]))
                    free(dve.tensor_copy(den[:, 4 * t + h:4 * t + h + 1], b[:, HD:HD + 1]), J(f"N{h}", t))

            mweights(0)
            mscores(0)
            for h in range(1, NH):
                mweights(h)
                mscores(h)
                mnumer(h - 1)
                if h == 2:
                    diagonals("lm")
            b = see(dve, J("lmr"))
            for k in range(ND):
                dve.wait_ge(S["conv_done"], k + 1)
                ins = TT(yc[:, k, :], yc[:, k, :], b, ALU.subtract)
                count("lv_sub", ins) if k < ND - 1 else free(ins, J("lmr"))
            dve.wait_ge(S["lv_sub"], 7)
            freed(dve, J("lmr"))
            mnumer(NH - 1)
            diagonals("lv")
            scale_tiles("lv", yc, lambda k: cv("cv_ln_g", k))
            steps2 = [0]

            def hstep(ins):
                steps2[0] += 1
                ins.then_inc(S["h_chain"], 1)
                dve.wait_ge(S["h_chain"], steps2[0])

            for t in range(NT):
                for h in range(NH):
                    freed(dve, J(f"N{h}", t))
            hstep(STT(fin, den, -1.0, den, ALU.mult, ALU.max))
            hstep(TT(fin, fin, emT, ALU.max))
            hstep(dve.reciprocal(fin, fin))
            dve.wait_ge(S["h_sq"], 16)
            hstep(TT(t16, ssq, fin, ALU.mult))
            hstep(TT(t16, t16, fin, ALU.mult))
            dve.wait_ge(S["h_sq"], 17)
            hstep(dve.reciprocal(t16, t16))
            hstep(TT(fin, fin, t16, ALU.mult))
            for j in range(8):
                freed(dve, J("o", j))
            for t in range(NT):
                for h in range(NH):
                    c = slice(HD * h, HD * h + HD)
                    count("h_done", STT(hn[:, t, c], hn[:, t, c], fin[:, 4 * t + h:4 * t + h + 1], og[:, t, c], ALU.mult, ALU.mult))
            see(dve, J("hT", 7))
            mod_sums(accB, 8)
            diagonals("n2")
            b = see(dve, J("modB"))
            free(TT(mod[:, 16:48], b[:, 0:32], vec[:, COL["ada_b"] + 16:COL["ada_b"] + 48], ALU.add), J("modB"))
            freed(dve, J("modB"))
            dve.sem_inc(S["mod_done"], 1)
            link(TT(gain[:, 8:16], mod[:, 16:24], vcols("mix_post_g", 8), ALU.mult))
            link(STT(gain[:, 16:24], mod[:, 32:40], 1.0, vcols("ffn_pre_g", 8), ALU.add, ALU.mult))
            link(TT(gain[:, 24:32], mod[:, 40:48], vcols("ffn_post_g", 8), ALU.mult))
            for k in range(ND):
                freed(dve, J("wo", k))
            residual("n2", 8)
            count("zeros_made", dve.memset(zeros, 0.0))
            diagonals("n3")
            dve.wait_ge(S["x_upd"], 8)
            scale_tiles("n3", uT, lambda k: gain[:, 16 + k:17 + k])
            for k in range(ND):
                dve.wait_ge(S["shifted"], SHIFTED["n3"] + k + 1)
                count("u_split", STT(uL[:, k, :], uT[:, k, :], mod[:, 24 + k:25 + k], uH[:, k, :].bitcast(F32), ALU.add, ALU.subtract))
            dve.wait_ge(S["pos_in"], 16)
            link(dve.tensor_copy(tA[:, 0, :], posI))
            MAGIC, C1 = 12582912.0, 6.28125
            C2 = float(np.float32(2 * np.pi - C1))
            C3 = float(2 * np.pi - C1 - np.float64(np.float32(2 * np.pi - C1)))
            for i in range(4):
                r, off = tA[:, 2 + i % 2, :], 0.25 * (i % 2 == 0)
                if i >= 2:
                    dve.wait_ge(S["trig_act"], i - 1)
                link(TS(tA[:, 1, :], tA[:, 0, :], const[:, 1344 + i // 2:1345 + i // 2], None, ALU.mult))
                link(TS(r, tA[:, 1, :], float(1 / (2 * np.pi)), off, ALU.mult, ALU.add))
                link(TS(r, r, MAGIC, None, ALU.add))
                link(TS(r, r, -MAGIC, None, ALU.add))
                link(STT(tA[:, 1, :], r, -C1, tA[:, 1, :], ALU.mult, ALU.add))
                link(STT(tA[:, 1, :], r, -C2, tA[:, 1, :], ALU.mult, ALU.add))
                link(STT(tA[:, 1, :], r, -C3, tA[:, 1, :], ALU.mult, ALU.add))
                link(TS(tA[:, 1, :], tA[:, 1, :], off * 2 * np.pi, 3.1415925, ALU.add, ALU.min))
                count("trig_dve", TS(r, tA[:, 1, :], -3.1415925, None, ALU.max))
                dve.wait_ge(S["trig_dve"], i + 1)
            steps3 = [0]

            def ffn_step(ins):
                steps3[0] += 1
                ins.then_inc(S["up_conv"], 1)
                dve.wait_ge(S["up_conv"], steps3[0])

            def f_low(p):
                for half in range(2):
                    dve.wait_ge(S["f_high"], 2 * p + half + 1)
                    count("f_split", TT(fL[:, 2 * p + half, :], fT[:, 2 * p + half, :], fH[:, 2 * p + half, :].bitcast(F32), ALU.subtract))

            for p in range(11):
                for j, half in ((0, 0), (0, 1), (1, 0), (1, 1)):
                    n = 4 * p + 2 * j + half
                    job, c, dst = J("up", n), NF * j + 2 * p + half, tA[:, 2 * j + half, :]
                    b = see(dve, job)
                    dve.wait_ge(S["up_affine"], n + 1)
                    for d in range(1, FC):
                        ins = STT(dst[:, d:T], b[:, 0:T - d], cv("ffn_conv_w", 2 * NF * (FC - 1 - d) + c), dst[:, d:T], ALU.mult, ALU.add)
                        ffn_step(ins) if d < FC - 1 else free(ins, job)
                if p > 0:
                    f_low(p - 1)
                for half in range(2):
                    dve.wait_ge(S["up_silu"], 2 * p + half + 1)
                    freed(dve, J("up", 4 * p + half))
                    count("f_done", TT(fT[:, 2 * p + half, :], tA[:, half, :], tA[:, 2 + half, :], ALU.mult))
            f_low(10)
            diagonals("n4")
            for k in range(ND):
                freed(dve, J("down", k))
            residual("n4", 24)
            diagonals("n5")
            dve.wait_ge(S["x_upd"], 16)
            scale_tiles("n5", uT, lambda k: cv("attn_norm_g_2", k))

            def gained(name, i, dst, g, sq_n, p=P, width=T):
                dve.wait_ge(S["sq_done"], sq_n)
                free(TS(dst, see(dve, J(name, i))[0:p, 0:width], g, None, ALU.mult), J(name, i))

            for j in range(2):
                gained("cq", j, cq[:, j, :], cv("mla_q_norm_g_2", j), SQ["cq"][0] + j + 1)
            gained("ckv", 0, ckv, cv("mla_kv_norm_g_2"), SQ["ck"][1])
            gained("kpe", 0, kpe, cv("mla_k_qk_g_2", 1, ROPE), SQ["kpe"][1], ROPE)
            freed(dve, J("kpe"))
            diagonals("cq")
            for j in range(2):
                freed(dve, J("cq", j))
            job = J("cqr")
            b = see(dve, job)
            count("scaled", TT(cq[:, 0, :], cq[:, 0, :], b, ALU.mult))
            free(TT(cq[:, 1, :], cq[:, 1, :], b, ALU.mult), job)
            diagonals("ck")
            freed(dve, J("ckv"))
            free(TT(ckv, ckv, see(dve, J("ckr")), ALU.mult), J("ckr"))
            dve.sem_inc(S["rope_done"], 1)
            for h in range(NH):
                gained("qn", h, qn[:, h, :], gain[:, 32:33], SQ["q"][0] + h + 1)
            for h in range(NH):
                gained("qr", h, tA[0:ROPE, h, :], gain[0:ROPE, 33:34], SQ["q"][0] + 5 + h, ROPE)
            for h in range(NH):
                gained("kn", h, kn[:, h, :], cv("mla_k_qk_g_2"), SQ["k"][0] + h + 1)

            def rotate(x, dst, rot, cos, sin, p):
                link(TT(tB[0:p, 0, :], x, cos, ALU.mult))
                free(TT(tB[0:p, 1, :], see(dve, rot)[0:p, :], sin, ALU.mult), rot)
                freed(dve, rot)
                TT(dst, tB[0:p, 0, :], tB[0:p, 1, :], ALU.add).then_inc(S["rope_done"], 1)
                rotated[0] += 1
                dve.wait_ge(S["rope_done"], rotated[0])

            rotated = [1]
            dve.wait_ge(S["trig_act"], 4)
            rotate(kpe, kpe, J("krot"), trig[0:ROPE, 2, :], trig[0:ROPE, 3, :], ROPE)
            for h in range(NH):
                freed(dve, J("qr", h))
                rotate(tA[0:ROPE, h, :], qr[:, h, :], J("qrot", h), trig[0:ROPE, 2, :], trig[0:ROPE, 3, :], ROPE)
            diagonals("q")
            diagonals("k")
            for h in range(NH):
                freed(dve, J("qn", h))
                b = see(dve, J("qR", h))
                link(TT(qn[:, h, :], qn[:, h, :], b, ALU.mult))
                free(TT(qr[:, h, :], qr[:, h, :], b[0:ROPE, :], ALU.mult), J("qR", h))
            for h in range(NH):
                freed(dve, J("kn", h))
                b = see(dve, J("kR", h))
                link(TT(kn[:, h, :], kn[:, h, :], b, ALU.mult))
                free(TT(kr[:, h, :], kpe, b[0:ROPE, :], ALU.mult), J("kR", h))

            def maxima(name, n, base):
                for t in range(NT):
                    b = see(dve, J(name, t))
                    count("att_max", dve.tensor_reduce(soft[:, 0, base + t:base + t + 1], b[:, 0:n or P * (t + 1)], AX, ALU.max, negate=True))

            def normalize(name, n, src, base):
                for t in range(NT):
                    c = base + t
                    freed(dve, J(name, t))
                    link(dve.reciprocal(soft[:, 2, c:c + 1], soft[:, 1, c:c + 1]))
                    width = n or P * (t + 1)
                    count("att_norm", TS(src[:, t, 0:width], src[:, t, 0:width], soft[:, 2, c:c + 1], None, ALU.mult))

            for h in range(NH):
                maxima(f"A{h}", 0, NT * h)
                normalize(f"A{h}", 0, att[h % 2], NT * h)
            for j in range(8):
                free(dve.tensor_copy(rqk[:, j, :], see(dve, J("rqk", j))), J("rqk", j))
            for j in range(8):
                freed(dve, J("rqk", j))
                rotate(rqk[:, j, :], rqk[:, j, :], J("rrot", j), trig[:, 0, :], trig[:, 1, :], P)
            dve.wait_ge(S["decay_in"], 16)
            for h in range(NH):
                if h < 2:
                    see(dve, J(f"AO{2 + h}"))
                else:
                    see(dve, J(f"RO{h - 2}"))
                for s in range(NT):
                    free(TT(attT[h % 2][:, s, 0:T - P * s], see(dve, J(f"R{h}", s))[:, 0:T - P * s], decay[:, h, 0:T - P * s], ALU.mult), J(f"R{h}", s))
                if h:
                    free(dve.tensor_copy(cat[:, 3 + h, :], see(dve, J(f"RO{h - 1}"))), J(f"RO{h - 1}"))
            free(dve.tensor_copy(cat[:, 7, :], see(dve, J("RO3"))), J("RO3"))
            diagonals("gm")
            for h in range(NH):
                freed(dve, J(f"RO{h}"))
                free(TT(cat[:, 4 + h, :], cat[:, 4 + h, :], see(dve, J("gmr", h)), ALU.subtract), J("gmr", h))
            diagonals("gv")
            for h in range(NH):
                freed(dve, J("gmr", h))
                dve.wait_ge(S["sq_done"], SQ["gv"][0] + h + 1)
                free(STT(cat[:, 4 + h, :], cat[:, 4 + h, :], cv("ret_gn_g_2", h), see(dve, J("gvr", h)), ALU.mult, ALU.mult), J("gvr", h))
            for h in range(NH):
                freed(dve, J("gvr", h))
                freed(dve, J("rg", h))
                count("ret_sub", TT(cat[:, 4 + h, :], cat[:, 4 + h, :], rg[:, h, :], ALU.mult))

            def add_out(name):
                for k in range(ND):
                    free(TT(xT[:, k, :], see(dve, J(name, k)), xT[:, k, :], ALU.add), J(name, k))

            add_out("wo2")
            diagonals("n6")
            for k in range(ND):
                freed(dve, J("wo2", k))
            scale_tiles("n6", uT, lambda k: cv("cross_norm_g_2", k))
            diagonals("nm")
            for k in range(4):
                freed(dve, J("memT", k))
            dve.wait_ge(S["sq_done"], SQ["nm"][1])
            scale_tiles("nm", memT, lambda k: cv("mem_norm_g_2", k), width=MEM)
            for k in range(ND):
                gained("xq", k, xq[:, k, :], gain[:, 34 + k % 2:35 + k % 2], SQ["xq"][0] + k + 1)
            for k in range(ND):
                gained("xk", k, xk[:, k, :], cv("cross_k_qk_g_2", k % 2), SQ["xk"][0] + k + 1, width=MEM)
            diagonals("xq")
            for h in range(NH):
                freed(dve, J("xq", 2 * h))
                freed(dve, J("xq", 2 * h + 1))
                b = see(dve, J("xqr", h))
                link(TT(xq[:, 2 * h, :], xq[:, 2 * h, :], b, ALU.mult))
                free(TT(xq[:, 2 * h + 1, :], xq[:, 2 * h + 1, :], b, ALU.mult), J("xqr", h))
            diagonals("xk")
            for h in range(NH):
                freed(dve, J("xk", 2 * h))
                freed(dve, J("xk", 2 * h + 1))
                b = see(dve, J("xkr", h))[:, 0:MEM]
                link(TT(xk[:, 2 * h, :], xk[:, 2 * h, :], b, ALU.mult))
                free(TT(xk[:, 2 * h + 1, :], xk[:, 2 * h + 1, :], b, ALU.mult), J("xkr", h))
            for h in range(NH):
                maxima(f"X{h}", MEM, 16 + NT * h)
                normalize(f"X{h}", MEM, xp[h % 2], 16 + NT * h)
            add_out("xo")
            diagonals("n7")
            for k in range(ND):
                freed(dve, J("xo", k))
            scale_tiles("n7", uT, lambda k: cv("moe_norm_g_2", k))
            n = [0]

            def R(ins, name=None):
                n[0] += 1
                ins.then_inc(S["route_dve"], 1)
                dve.wait_ge(S["route_dve"], n[0])
                if name:
                    mark[name] = n[0]

            iota = const[:, 1352:1480]
            R(dve.tensor_copy(r_Lb, see(dve, J("bias"))[:, 0:36]))
            dve.sem_inc(bank_free[J("bias").bank], 1)
            R(dve.tensor_copy(r_L, see(dve, J("logit"))[:, 0:144].rearrange("p (t c) -> p t c", t=NT)))
            dve.sem_inc(bank_free[J("logit").bank], 1)
            four = lambda lo, *sh: scratch(lo, *sh)

            def bc(ap, shape):
                return ap.to_broadcast(shape)

            def first_largest(src, num, dst, lo):
                mx, eq = four(lo, NT, 1), four(lo + 8, NT, num)
                R(dve.tensor_reduce(mx[:, :, 0], src, AX, ALU.max))
                R(TT(eq, src, bc(mx, [P, NT, num]), ALU.is_equal))
                R(TT(eq, eq, bc(r_im[:, 0:num].unsqueeze(1), [P, NT, num]), ALU.mult))
                R(dve.tensor_reduce(mx[:, :, 0], eq, AX, ALU.min))
                R(TT(dst, bc(r_im[:, 0:num].unsqueeze(1), [P, NT, num]), bc(mx, [P, NT, num]), ALU.is_equal))

            R(TS(r_im, iota[:, 0:64], -64.0, None, ALU.add))
            gl, el_all = r_L[:, :, 0:NG], r_L[:, :, NG:NG + NE].rearrange("p t (g e) -> p t g e", g=NG)
            gb, oh_g = four(3000, NT, NG), four(3020, NT, NG)
            R(TT(gb, gl, bc(r_Lb[:, 0:NG].unsqueeze(1), [P, NT, NG]), ALU.add))
            first_largest(gb, NG, oh_g, 3040)
            gm_ = four(3120, NT, 1)
            R(dve.tensor_reduce(gm_[:, :, 0], gl, AX, ALU.max))
            R(TT(r_x, gl, bc(gm_, [P, NT, NG]), ALU.subtract), "group")
            big, el, eb_ = four(3200, NT, NG, EG), four(3400, NT, EG), four(3440, NT, EG)
            for src, dst in ((el_all, el), (bc(r_Lb[:, NG:NG + NE].rearrange("p (g e) -> p g e", g=NG).unsqueeze(1), [P, NT, NG, EG]), eb_)):
                R(TT(big, src, bc(oh_g.unsqueeze(3), [P, NT, NG, EG]), ALU.mult))
                R(dve.tensor_reduce(dst, big.rearrange("p t g e -> p t e g"), AX, ALU.add))
            R(TT(eb_, el, eb_, ALU.add))
            R(dve.tensor_reduce(gm_[:, :, 0], el, AX, ALU.max))
            R(TT(r_y, el, bc(gm_, [P, NT, EG]), ALU.subtract), "expert")
            oh = [four(3480, NT, EG), four(3520, NT, EG)]
            first_largest(eb_, EG, oh[0], 3560)
            R(STT(eb_, oh[0], 2 * NEG, eb_, ALU.mult, ALU.add))
            first_largest(eb_, EG, oh[1], 3560)
            gsum, gw, pk, psum_ = four(3620, NT, 1), four(3624, NT, 1), [four(3628, NT, 1), four(3632, NT, 1)], four(3636, NT, 1)
            dve.wait_ge(S["route_act"], 1)
            R(dve.tensor_reduce(gsum[:, :, 0], r_x, AX, ALU.add))
            R(TT(gb, r_x, oh_g, ALU.mult))
            R(dve.tensor_reduce(gw[:, :, 0], gb, AX, ALU.add))
            R(dve.reciprocal(gsum, gsum))
            R(TT(gw, gw, gsum, ALU.mult))
            dve.wait_ge(S["route_act"], 2)
            t8 = four(3640, NT, EG)
            for c in range(2):
                R(TT(t8, r_y, oh[c], ALU.mult))
                R(dve.tensor_reduce(pk[c][:, :, 0], t8, AX, ALU.add))
            R(TT(psum_, pk[0], pk[1], ALU.add))
            R(dve.reciprocal(psum_, psum_))
            R(TT(psum_, psum_, gw, ALU.mult))
            for c in range(2):
                R(TT(share[:, 4 * c:4 * c + 4].unsqueeze(2), pk[c], psum_, ALU.mult))
            for c in range(2):
                R(TT(r_E[c], bc(oh_g.unsqueeze(3), [P, NT, NG, EG]), bc(oh[c].unsqueeze(2), [P, NT, NG, EG]), ALU.mult))
            flatE = [scratch(500 + 128 * c, NT, NE) for c in range(2)]
            R(TT(r_M, flatE[0], flatE[1], ALU.add), "M")
            b = see(dve, J("rank"))
            rank, cnt, nb, end, first = four(3700, NT, NE), four(3830, NE), four(3870, NE), four(3910, NE), four(3950, NE)
            R(dve.tensor_copy(scratch(3700, 160), b[:, 0:160]))
            cnt = scratch(3700, 160)[:, 128:160]
            R(TS(nb, cnt, 0.0, None, ALU.is_gt))
            for j in range(1, NT):
                R(STT(nb, cnt, float(P * j), nb, ALU.is_gt, ALU.add))
            onesrow = four(3990, NE)
            R(dve.memset(onesrow, 1.0))
            R(dve.tensor_tensor_scan(end, onesrow, nb, 0.0, ALU.mult, ALU.add))
            R(TT(first, end, nb, ALU.subtract))
            rk, q_, blk, bst, rowf = (four(4040 + 8 * i, NT, 1) for i in range(5))
            t32 = four(4100, NT, NE)
            for c in range(2):
                R(TT(t32, rank, flatE[c], ALU.mult))
                R(dve.tensor_reduce(rk[:, :, 0], t32, AX, ALU.add))
                R(TT(t32, bc(first.unsqueeze(1), [P, NT, NE]), flatE[c], ALU.mult))
                R(dve.tensor_reduce(bst[:, :, 0], t32, AX, ALU.add))
                R(TS(q_, rk, float(P), None, ALU.is_ge))
                for j in range(2, NT):
                    R(STT(q_, rk, float(P * j), q_, ALU.is_ge, ALU.add))
                R(TT(blk, bst, q_, ALU.add))
                R(STT(rk, q_, -float(P), rk, ALU.mult, ALU.add))
                R(STT(rowf, blk, float(P), rk, ALU.mult, ALU.add))
                R(dve.tensor_copy(row_of[:, 4 * c:4 * c + 4].unsqueeze(2), rowf))
                for t in range(NT):
                    i = NT * c + t
                    R(TS(r_A[:, i, :], iota, rk[:, t, :], None, ALU.is_equal))
                    R(TS(r_B[:, i, :], iota[:, 0:NBX], blk[:, t, :], const[:, 1348 + t:1349 + t], ALU.is_equal, ALU.mult))
            mark["AB"] = n[0]
            cmp_ = scratch(4300, NBX, NE)
            R(TT(cmp_, bc(end.unsqueeze(1), [P, NBX, NE]), bc(iota[:, 0:NBX].unsqueeze(2), [P, NBX, NE]), ALU.is_le))
            ef = four(4240, NBX)
            R(dve.tensor_reduce(ef, cmp_, AX, ALU.add))
            R(TS(ef, ef, float(NE - 1), None, ALU.min))
            R(dve.tensor_copy(expert_of, ef[0:1, :]))
            R(TS(ef[0:1, 0:NB // SLOTS], r_im[0:1, 0:NB // SLOTS], float(SLOTS), float(64 * SLOTS), ALU.mult, ALU.add))
            R(TT(ef[0:1, 0:NB // SLOTS], ef[0:1, 0:NB // SLOTS], bc(end[0:1, NE - 1:NE], [1, NB // SLOTS]), ALU.is_lt))
            R(dve.tensor_reduce(ef[0:1, 12:13], ef[0:1, 0:NB // SLOTS], AX, ALU.add))
            R(dve.tensor_copy(turn_count, ef[0:1, 12:13]))
            dve.tensor_copy(token_of, see(dve, J("tab"))[:, 0:NBX]).then_inc(S["table_ready"], 1)
            def dve_turn(s, n):
                dve.wait_ge(moe_full[1], n + 3)
                dve.tensor_copy(xgT[s % 2][:, 4:8, :], bank[1].rearrange("p (k t) -> p k t", k=4)).then_inc(moe_free[1], 1)

            dve_turn(0, 0)
            for i in rep(dve, turns_of(dve)):
                for s in range(SLOTS):
                    m = i * SLOTS + s
                    dve.wait_ge(S["g_silu"], m + 1)
                    TT(act_m[s % 2], bank[2 + s % 2][:, EF:2 * EF], act_f[s % 2], ALU.mult).then_inc(S["act_done"], 1)
                    dve_turn(s + 1, m + 1)
                    dve.wait_ge(moe_full[4], m + 1)
                    dve.tensor_copy(actT[s % 2], bank[4][:, 0:2 * P].rearrange("p (j t) -> p j t", j=2)).then_inc(moe_free[4], 1)
                    dve.wait_ge(moe_full[6], m + 1 + SLOTS)
                    dve.wait_ge(y_out[s % 2], 16 * (i * 2 + s // 2 + 1))
                    dve.tensor_copy(yb[s % 2][:, 512:1024], bank[6]).then_inc(moe_free[6], 1)
            for t in range(NT):
                for c in range(2):
                    k = 2 * t + c
                    dve.wait_ge(picked[k % 4], 16 * (k // 4 + 1))
                    ins = STT(xoutTM[:, t, :], pick[k % 4], share[:, 4 * c + t:4 * c + t + 1], xoutTM[:, t, :], ALU.mult, ALU.add)
                    ins.then_inc(S["out_sum"], 1)
                    dve.wait_ge(S["out_sum"], k + 1)

        @block.gpsimd
        def _(pool):
            pool.memset(v1[:, :, :, HD:HD + 1], 1.0).then_inc(S["vone_done"], 1)
            for b in range(8):
                pool.sem_inc(bank_free[b], 1)
            for b in range(7):
                pool.sem_inc(moe_free[b], 1)
            pool.sem_inc(S["act_done"], 2)
            pool.wait_ge(S["const_in"], 16)
            for h in range(NH):
                for s in range(NT):
                    pool.wait_ge(S["w_exp"], NT * h + s + 1)
                    pool.tensor_tensor(tA[:, s, 0:P], tA[:, s, 0:P], tri, ALU.mult).then_inc(S["w_mask"], 1)
            for i, n in enumerate(split_panels):
                raw, high, low = panel_parts(n)
                pool.wait_ge(S["panel_high"], i + 1)
                pool.tensor_tensor(low, raw, high.bitcast(F32), ALU.subtract).then_inc(S["panel_split"], 1)
            pool.wait_ge(S["hm_out"], 16)
            pool.wait_ge(S["table_ready"], 1)
            pool.sem_inc(moe_full[1], 2)
            turns = turns_of(pool)

            def gather(s, m):
                pool.wait_ge(moe_full[1], m + 1)
                pool.sem_inc(S["gather_go"], 1)
                pool.tensor_copy(index[s % 2], token_of[:, bass.ds(m, 1)]).then_inc(S["index_done"], 1)
                pool.wait_ge(S["index_done"], m + 1)
                pool.sem_inc(S["gather_go"], 1)
                pool.indirect_dma_start(xg[s % 2], None, hm_dram, bass.IndirectOffsetOnAxis(ap=index[s % 2].bitcast(U32), axis=0)).then_inc(gathered[s % 2], 16)

            for i in rep(pool, turns):
                for s in range(SLOTS):
                    gather(s, i * SLOTS + s)
            gather(0, turns * SLOTS)
            for b in range(2):
                pool.wait_ge(y_out[b], turns * 32 + 16)
                pool.sem_inc(S["gather_go"], 1)
            for k in range(2 * NT):
                t, c = k // 2, k % 2
                if k >= 4:
                    pool.wait_ge(S["out_sum"], k - 3)
                pool.indirect_dma_start(pick[k % 4], None, y_dram, bass.IndirectOffsetOnAxis(ap=row_of[:, 4 * c + t:4 * c + t + 1].bitcast(U32), axis=0)).then_inc(picked[k % 4], 16)

        @block.sync
        def _(sp):
            sp.dma_start(const, w["const"][:, 0:CW]).then_inc(S["const_in"], 16)
            sp.dma_start(xTM, w["x"].rearrange("(t p) d -> p t d", p=P)).then_inc(S["x_in"], 16)
            for n, (src, _, _) in enumerate(panels):
                if n >= SLOTS:
                    name, i = panels[n - SLOTS][1]
                    if name == "mod":
                        sp.wait_ge(S["mod_acc"], i + 1)
                    elif name == "part":
                        sp.wait_ge(S["part_read"], i + 1)
                    else:
                        see(sp, J(name, i))
                k, width = src.shape[0] // P, src.shape[1]
                dst = ring[:, PANEL * (n % SLOTS):PANEL * (n % SLOTS) + k * width].rearrange("p (k c) -> p k c", k=k)
                sp.dma_start(dst, src.rearrange("(k p) c -> p k c", p=P)).then_inc(ring_full[n % SLOTS], 16)
            sp.wait_ge(S["table_ready"], 1)
            wge, wue, wde = w["expert_w_gate_2"], w["expert_w_up_2"], w["expert_w_down_2"]
            for i in rep(sp, turns_of(sp)):
                for s in range(SLOTS):
                    e = sp.value_load(expert_of[0:1, bass.ds(i * SLOTS + s, 1)], min_val=0, max_val=NE - 1)
                    sp.wait_ge(moe_full[6], i * SLOTS + s + 1)
                    for src, dst in ((wge, wgu[s][:, :, 0:EF]), (wue, wgu[s][:, :, EF:2 * EF]), (wde, wdn[s])):
                        sp.dma_start(dst, src[bass.ds(e, 1)].rearrange("e (k p) f -> p (e k) f", p=P)).then_inc(moe_w[s], 16)

        @block.tensor
        def _(pe):
            np_ = [0]

            def next_panel():
                while panels[np_[0]][1][0] == "mod":
                    np_[0] += 1
                np_[0] += 1
                return np_[0] - 1

            def panel():
                n = next_panel()
                src = panels[n][0]
                k, width = src.shape[0] // P, src.shape[1]
                pe.wait_ge(ring_full[n % SLOTS], 16 * (n // SLOTS + 1))
                return ring[:, PANEL * (n % SLOTS):PANEL * (n % SLOTS) + k * width].rearrange("p (k c) -> p k c", k=k)

            splits = [0]

            def parts():
                n = next_panel()
                splits[0] += 1
                pe.wait_ge(S["panel_split"], splits[0])
                return [x.rearrange("p (k c) -> p k c", c=P) for x in panel_parts(n)[1:]]

            def triple(job, wH, wL, xH, xL, first, final):
                pe.matmul(bank[job.bank], wH, xH, start=first, stop=False)
                pe.matmul(bank[job.bank], wH, xL, start=False, stop=False)
                return pe.matmul(bank[job.bank], wL, xH, start=False, stop=final)

            def product(job, pairs, cols=slice(0, 512), p=P, last=True):
                for k, (a, b) in enumerate(pairs):
                    m = pe.matmul(bank[job.bank][0:p, cols], a, b, start=(k == 0), stop=(k == len(pairs) - 1))
                if last:
                    full(m, job)

            def stats(name, tile_of):
                sizes, nt, _, kind = NORMS[name]
                job = J(name + "s")
                opened(job)
                i = 0
                for g, size in enumerate(sizes):
                    for k in range(size):
                        if kind == "rms":
                            pe.wait_ge(S["sq_done"], SQ[name][0] + k + 1 if len(sizes) == 1 else SQ[name][1])
                        a = tile_of(g, k)
                        r = a.shape[0]
                        for t in range(nt):
                            m = pe.matmul(bank[job.bank][:, g * nt + t:g * nt + t + 1], a[:, P * t:P * t + P], ones[0:r, 0:1],
                                          start=(i == 0 and t == 0), stop=(k == size - 1), skip_group_check=True)
                        i += 1
                full(m, job)

            def spread(name, g=0):
                nt = NORMS[name][1]
                i = DIAG[name] + g
                pe.wait_ge(S["diag_done"], i + 1)
                job = J(RJOB[name], g)
                opened(job)
                full(pe.matmul(bank[job.bank][:, 0:nt * P], ones, dg[:, i % 2, 0:nt * P], start=True, stop=True), job)

            def wait_u(name, k, n=ND):
                if name in SHIFTED:
                    pe.wait_ge(S["shifted"], SHIFTED[name] + k + 1)
                elif k < n - 1:
                    pe.wait_ge(S["scaled"], SCALED[name] + k + 1)
                else:
                    freed(pe, J(RJOB[name]))

            def linear(job, wp, lo, width, src, uname=None, p=P):
                opened(job)
                nk = wp.shape[1]
                for k in range(nk):
                    if uname:
                        wait_u(uname, k, nk)
                    m = pe.matmul(bank[job.bank][0:p, :src.shape[2]], wp[:, k, lo:lo + width], src[:, k, :], start=(k == 0), stop=(k == nk - 1))
                full(m, job)

            pe.wait_ge(S["const_in"], 16)
            pe.wait_ge(S["vec_in"], 16 * len(vector_rows))
            for j in range(2):
                job = J("vec", j)
                opened(job)
                gs = list(range(VG))[4 * j:4 * j + 4]
                for q, g in enumerate(gs):
                    m = pe.transpose(bank[job.bank][:, P * q:P * q + P], vrows[:, g, :], ident)
                full(m, job)
            pe.wait_ge(S["x_in"], 16)
            for k in range(ND):
                job = J("xT", k)
                opened(job)
                for t in range(NT):
                    m = pe.transpose(bank[job.bank][:, P * t:P * t + P], xTM[:, t, P * k:P * k + P], ident)
                full(m, job)
            stats("n1", lambda g, k: sq[:, k, :])

            def modulation(name, acc, first):
                job = J(name)
                opened(job)
                for q in range(acc.shape[1]):
                    pe.wait_ge(S["mod_acc"], first + q + 1)
                    for half in range(2):
                        m = pe.matmul(bank[job.bank][:, 2 * q + half:2 * q + half + 1], acc[:, q, P * half:P * half + P], ones[:, 0:1],
                                      start=True, stop=True)
                full(m, job)

            modulation("modA", accA, 0)
            spread("n1")
            for p in range(4):
                for j, half in ((0, 0), (0, 1), (1, 0), (1, 1)):
                    if half == 0:
                        wp = panel()
                    linear(J("glu", 4 * p + 2 * j + half), wp, P * half, P, uT, "n1" if p == 0 else None)
            pe.wait_ge(S["wg_in"], 48)
            for j in range(2):
                job = J("gates", j)
                opened(job)
                for k in range(ND):
                    m = pe.matmul(bank[job.bank][0:4, :], wg[:, 8 * k + 4 * j:8 * k + 4 * j + 4], uT[:, k, :], start=(k == 0), stop=(k == ND - 1))
                full(m, job)
            for p in range(8):
                wp = panel()
                for half in range(2):
                    linear(J("qk", 2 * p + half), wp, P * half, P, uT)

            def tokens_major(name, count, nt_per, src, srck=ND):
                for p in range(count):
                    wp = panel()
                    for half in range(nt_per // 2):
                        job = J(name, p * (nt_per // 2) + half)
                        opened(job)
                        for q in range(2):
                            t = 2 * half + q
                            for k in range(ND):
                                m = pe.matmul(bank[job.bank][:, 256 * q:256 * q + 256], src[:, k, P * t:P * t + P], wp[:, k, :],
                                              start=(k == 0), stop=(k == ND - 1))
                        full(m, job)

            tokens_major("v", 4, NT, uT)
            job = J("gT")
            opened(job)
            pe.wait_ge(S["gate_dve"], GD_M)
            pe.wait_ge(S["gate_act"], GA_EM)
            for i, nm in enumerate(("a", "em")):
                for t in range(NT):
                    m = pe.transpose(bank[job.bank][:, 16 * i + 4 * t:16 * i + 4 * t + 4], rows[nm][:, P * t:P * t + P], ident[0:4, 0:4])
            full(m, job)
            freed(pe, J("gT"))
            tokens_major("o", 4, NT, uT)

            def mb(h):
                product_open(J(f"Mb{h}"))
                product(J(f"Mb{h}"), [(sel[h], Mrow)])

            def product_open(job):
                opened(job)

            def scores(h):
                for s in range(NT):
                    job = J(f"S{h}", s)
                    opened(job)
                    if h == 0 and s == 0:
                        pe.wait_ge(S["qk_done"], 16)
                    product(job, [(qk[:, 8 + 2 * h + c, P * s:P * s + P], qk[:, 2 * h + c, P * s:T]) for c in range(2)],
                            slice(0, T - P * s))

            def numer(h):
                for t in range(NT):
                    job = J(f"N{h}", t)
                    opened(job)
                    for s in range(t + 1):
                        freed(pe, J(f"S{h}", s))
                    if h == 0 and t == 0:
                        pe.wait_ge(S["vone_done"], 1)
                        for p in range(8):
                            freed(pe, J("v", p))
                    product(job, [(prob[h % 2][:, s, P * (t - s):P * (t - s) + P], v1[:, s, h, :]) for s in range(t + 1)],
                            slice(0, HD + 1))

            mb(0)
            scores(0)
            for h in range(1, NH):
                mb(h)
                scores(h)
                numer(h - 1)
                if h == 2:
                    pe.wait_ge(S["conv_done"], 8)
                    stats("lm", lambda g, k: yc[:, k, :])
                if h == 3:
                    spread("lm")
            numer(NH - 1)
            stats("lv", lambda g, k: sq[:, k, :])
            spread("lv")
            wo_panels = []
            for k in range(4):
                wo_panels.append(panel())
                opened(J("wo", k))
                for c in range(8, 16):
                    if k == 0:
                        pe.wait_ge(S["lv_done"], c - 7)
                    pe.matmul(bank[J("wo", k).bank], wo_panels[k][:, c, :], yc[:, c - 8, :], start=(c == 8), stop=False)
            for k in range(ND):
                job = J("hT", k)
                opened(job)
                for t in range(NT):
                    pe.wait_ge(S["h_done"], NH * t + k // 2 + 1)
                    m = pe.transpose(bank[job.bank][:, P * t:P * t + P], hn[:, t, P * k:P * k + P], ident)
                full(m, job)
            for k in range(4):
                for c in range(8):
                    if k == 0:
                        freed(pe, J("hT", c))
                    m = pe.matmul(bank[J("wo", k).bank], wo_panels[k][:, c, :], hT[:, c, :], start=False, stop=(c == 7))
                full(m, J("wo", k))
            for k in range(4, 8):
                wp = panel()
                opened(J("wo", k))
                for c in range(16):
                    m = pe.matmul(bank[J("wo", k).bank], wp[:, c, :], hT[:, c, :] if c < 8 else yc[:, c - 8, :], start=(c == 0), stop=(c == 15))
                full(m, J("wo", k))
            stats("n2", lambda g, k: sq[:, k, :])
            modulation("modB", accB, 8)
            spread("n2")
            stats("n3", lambda g, k: sq[:, k, :])
            spread("n3")
            for n in range(44):
                job = J("up", n)
                opened(job)
                wH, wL = parts()
                for k in range(ND):
                    if n == 0:
                        pe.wait_ge(S["u_split"], k + 1)
                    m = triple(job, wH[:, k, :], wL[:, k, :], uH[:, k, :], uL[:, k, :], k == 0, k == ND - 1)
                full(m, job)
            for k in range(8):
                job = J("down", k)
                opened(job)
                for i, (lo, hi) in enumerate(DOWN_PARTS):
                    wH, wL = parts()
                    for c in range(lo, hi):
                        if k == 0:
                            pe.wait_ge(S["f_split"], c + 1)
                        m = triple(job, wH[:, c - lo, :], wL[:, c - lo, :], fH[:, c, :], fL[:, c, :], c == 0, c == NF - 1)
                    if i < 2:
                        m.then_inc(S["part_read"], 1)
                full(m, job)
            stats("n4", lambda g, k: sq[:, k, :])
            spread("n4")
            stats("n5", lambda g, k: sq[:, k, :])
            spread("n5")
            wp = panel()
            for j in range(2):
                linear(J("cq", j), wp, P * j, P, uT, "n5")
            wp = panel()
            linear(J("ckv"), wp, 0, P, uT)
            linear(J("kpe"), wp, P, ROPE, uT, p=ROPE)
            stats("cq", lambda g, k: sq[:, k, :])
            spread("cq")
            stats("ck", lambda g, k: sq[:, 2, :])
            spread("ck")
            wuq = panel()
            wukv = panel()
            for h in range(NH):
                linear(J("qn", h), wuq, QKD * h, NOPE, cq, "cq" if h == 0 else None)
            for h in range(NH):
                linear(J("qr", h), wuq, QKD * h + NOPE, ROPE, cq, p=ROPE)
            freed(pe, J("ckr"))
            ck3 = ckv.unsqueeze(1)
            for h in range(NH):
                linear(J("kn", h), wukv, 256 * h, NOPE, ck3)
            for t in range(NT):
                job = J("mv", t)
                opened(job)
                full(pe.matmul(bank[job.bank], ckv[:, P * t:P * t + P], wukv[:, 0, :].rearrange("p (h c) -> p h c", h=NH)[:, :, 128:256],
                               start=True, stop=True), job)
            freed(pe, J("kpe"))
            opened(J("krot"))
            pe.wait_ge(S["rope_done"], 1)
            product(J("krot"), [(rot64, kpe)], p=ROPE)
            for h in range(NH):
                opened(J("qrot", h))
                pe.wait_ge(S["rope_done"], 2 + h)
                product(J("qrot", h), [(rot64, tA[0:64, h, :])], p=ROPE)
            stats("q", lambda g, k: qsq(g, k))
            stats("k", lambda g, k: ksq(g, k))
            for g in range(NH):
                spread("q", g)
            for g in range(NH):
                spread("k", g)
            def att_scores(h):
                for t in range(NT):
                    job = J(f"A{h}", t)
                    opened(job)
                    if h == 0 and t == 0:
                        for g in range(NH):
                            freed(pe, J("qR", g))
                            freed(pe, J("kR", g))
                    n = P * (t + 1)
                    pe.matmul(bank[job.bank][:, 0:n], qn[:, h, P * t:P * t + P], kn[:, h, 0:n], start=True, stop=False)
                    pe.matmul(bank[job.bank][:, n - P:n], ident, neg, start=False, stop=False, skip_group_check=True)
                    full(pe.matmul(bank[job.bank][:, 0:n], qr[:, h, P * t:P * t + P], kr[:, h, 0:n], start=False, stop=True), job)

            def att_out(h):
                for s in range(NT):
                    job = J(f"AT{h}", s)
                    opened(job)
                    for t in range(s, NT):
                        pe.wait_ge(S["att_norm"], NT * h + t + 1)
                        m = pe.transpose(bank[job.bank][:, P * t:P * t + P], att[h % 2][:, t, P * s:P * s + P], ident)
                    full(m, job)
                job = J(f"AO{h}")
                opened(job)
                for s in reversed(range(NT)):
                    freed(pe, J(f"AT{h}", s))
                    if h == 0:
                        freed(pe, J("mv", s))
                    m = pe.matmul(bank[job.bank][:, P * s:T], mv[:, s, P * h:P * h + P], attT[h % 2][:, s, P * s:T],
                                  start=(s == NT - 1), stop=(s == 0), skip_group_check=True)
                full(m, job)

            for h in range(NH + 1):
                if h < NH:
                    att_scores(h)
                if h > 0:
                    att_out(h - 1)
            for p in range(4):
                wp = panel()
                for half in range(2):
                    linear(J("rqk", 2 * p + half), wp, P * half, P, uT)
            for j in range(8):
                freed(pe, J("rqk", j))
                opened(J("rrot", j))
                product(J("rrot", j), [(rot128, rqk[:, j, :])])
            tokens_major("rv", 2, NT, uT)
            for p in range(2):
                wp = panel()
                for half in range(2):
                    linear(J("rg", 2 * p + half), wp, P * half, P, uT)
            def ret_scores(h):
                for s in range(NT):
                    job = J(f"R{h}", s)
                    opened(job)
                    if s == 0:
                        pe.wait_ge(S["rope_done"], RD_R + 4 + h + 1)
                    product(job, [(rqk[:, 4 + h, P * s:P * s + P], rqk[:, h, P * s:T])], slice(0, T - P * s))

            def ret_out(h):
                job = J(f"RO{h}")
                opened(job)
                for s in reversed(range(NT)):
                    freed(pe, J(f"R{h}", s))
                    if h == 0:
                        freed(pe, J("rv", s))
                    m = pe.matmul(bank[job.bank][:, P * s:T], rv[:, s, P * h:P * h + P], attT[h % 2][:, s, 0:T - P * s],
                                  start=(s == NT - 1), stop=(s == 0), skip_group_check=True)
                full(m, job)

            for h in range(NH + 1):
                if h < NH:
                    ret_scores(h)
                if h > 0:
                    ret_out(h - 1)
            for h in range(NH):
                freed(pe, J(f"RO{h}"))
            stats("gm", lambda g, k: cat[:, 4 + g, :])
            for g in range(NH):
                spread("gm", g)
            stats("gv", lambda g, k: sq[:, g, :])
            for g in range(NH):
                spread("gv", g)
            for p in range(4):
                wp = panel()
                for half in range(2):
                    job = J("wo2", 2 * p + half)
                    opened(job)
                    for k in range(ND):
                        if p == 0:
                            if k < 4:
                                freed(pe, J(f"AO{k}"))
                            else:
                                pe.wait_ge(S["ret_sub"], k - 3)
                        m = pe.matmul(bank[job.bank], wp[:, k, P * half:P * half + P], cat[:, k, :], start=(k == 0), stop=(k == 7))
                    full(m, job)
            stats("n6", lambda g, k: sq[:, k, :])
            spread("n6")
            pe.wait_ge(S["mem_in"], 16)
            for kk in range(4):
                job = J("memT", kk)
                opened(job)
                for q in range(2):
                    for m2 in range(NM):
                        k = 2 * kk + q
                        m = pe.transpose(bank[job.bank][:, MEM * q + P * m2:MEM * q + P * m2 + P], memTM[:, m2, P * k:P * k + P], ident)
                full(m, job)
            stats("nm", lambda g, k: sq[:, k, 0:MEM])
            spread("nm")
            for p in range(4):
                wp = panel()
                for half in range(2):
                    linear(J("xq", 2 * p + half), wp, P * half, P, uT, "n6" if p == 0 else None)
            for p in range(4):
                wp = panel()
                for half in range(2):
                    linear(J("xk", 2 * p + half), wp, P * half, P, memT, "nm" if p == 0 else None)
            tokens_major("xv", 4, NM, memT)
            stats("xq", lambda g, k: sq[:, 2 * g + k, :])
            for g in range(NH):
                spread("xq", g)
            stats("xk", lambda g, k: xksq[:, 2 * g + k, :])
            for g in range(NH):
                spread("xk", g)
            def cross_scores(h):
                freed(pe, J("xqr", h))
                freed(pe, J("xkr", h))
                for t in range(NT):
                    job = J(f"X{h}", t)
                    opened(job)
                    product(job, [(xq[:, 2 * h + c, P * t:P * t + P], xk[:, 2 * h + c, :]) for c in range(2)], slice(0, MEM))

            def cross_out(h):
                for m2 in range(NM):
                    job = J(f"XT{h}", m2)
                    opened(job)
                    for t in range(NT):
                        pe.wait_ge(S["att_norm"], 16 + NT * h + t + 1)
                        m = pe.transpose(bank[job.bank][:, P * t:P * t + P], xp[h % 2][:, t, P * m2:P * m2 + P], ident)
                    full(m, job)
                for half in range(2):
                    job = J(f"XO{h}", half)
                    opened(job)
                    for m2 in range(NM):
                        freed(pe, J(f"XT{h}", m2))
                    if h == 0:
                        for q in range(4):
                            freed(pe, J("xv", q))
                    product(job, [(xv[:, m2, HD * h + P * half:HD * h + P * half + P], xpT[h % 2][:, m2, :]) for m2 in range(NM)])

            for h in range(NH + 1):
                if h < NH:
                    cross_scores(h)
                if h > 0:
                    cross_out(h - 1)
            for p in range(4):
                wp = panel()
                for half in range(2):
                    job = J("xo", 2 * p + half)
                    opened(job)
                    for k in range(ND):
                        if p == 0:
                            freed(pe, J(f"XO{k // 2}", k % 2))
                        m = pe.matmul(bank[job.bank], wp[:, k, P * half:P * half + P], xoT[:, k, :], start=(k == 0), stop=(k == 7))
                    full(m, job)
            stats("n7", lambda g, k: sq[:, k, :])
            spread("n7")
            pe.wait_ge(S["rt_in"], 64)
            job = J("bias")
            opened(job)
            product(job, [(ones[0:1, :], bias_row)], slice(0, 36))
            job = J("logit")
            opened(job)
            for t in range(NT):
                for k in range(ND):
                    wait_u("n7", k)
                    m = pe.matmul(bank[job.bank][:, 36 * t:36 * t + 36], uT[:, k, P * t:P * t + P], wr[:, k, :], start=(k == 0), stop=(k == 7),
                                  skip_group_check=True)
            full(m, job)
            for name, src in (("hmT", uT), ("xTM", xT)):
                for j in range(8):
                    job = J(name, j)
                    opened(job)
                    t, half = j // 2, j % 2
                    for q in range(4):
                        m = pe.transpose(bank[job.bank][:, P * q:P * q + P], src[:, 4 * half + q, P * t:P * t + P], ident)
                    full(m, job)
            job = J("rank")
            opened(job)
            pe.wait_ge(S["route_dve"], mark["M"])
            for t in range(NT + 1):
                parts = [(ones, r_M[:, s, :]) for s in range(t)] + ([(below, r_M[:, t, :])] if t < NT else [])
                for k, (a, b) in enumerate(parts):
                    m = pe.matmul(bank[job.bank][:, 32 * t:32 * t + 32], a, b, start=(k == 0), stop=(k == len(parts) - 1), skip_group_check=True)
            full(m, job)
            job = J("tab")
            opened(job)
            pe.wait_ge(S["route_dve"], mark["AB"])
            for i in range(8):
                m = pe.matmul(bank[job.bank][:, 0:NBX], r_A[:, i, :], r_B[:, i, :], start=(i == 0), stop=(i == 7))
            full(m, job)
            pe.wait_ge(S["table_ready"], 1)
            for job in LAST:
                freed(pe, job)
            pe.sem_inc(moe_full[6], SLOTS)

            def turn(i, s, ahead=0):
                n = i * SLOTS + s
                pe.wait_ge(gathered[s % 2], 16 * (i * 2 + s // 2 + 1))
                for half in range(2):
                    pe.wait_ge(moe_free[half], n + 1)
                    for q in range(4):
                        m = pe.transpose(bank[half][:, P * q:P * q + P], xg[s % 2][:, P * (4 * half + q):P * (4 * half + q) + P], ident)
                    m.then_inc(moe_full[half], 1)

            turn(0, 0)
            for i in rep(pe, turns_of(pe)):
                for s in range(SLOTS):
                    n = i * SLOTS + s
                    pe.wait_ge(S["act_done"], n + 1)
                    pe.wait_ge(moe_w[s], 48 * i + 48)
                    for half in range(2):
                        pe.wait_ge(moe_free[half], n + 2)
                        for k in range(4 * half, 4 * half + 4):
                            m = pe.matmul(bank[2 + s % 2], xgT[s % 2][:, k, :], wgu[s][:, k, :], start=(k == 0), stop=(k == 7))
                    m.then_inc(moe_full[2 + s % 2], 1)
                    turn(i, s + 1)
                    pe.wait_ge(S["act_done"], n + 3)
                    pe.wait_ge(moe_free[4], n + 1)
                    for j in range(2):
                        m = pe.transpose(bank[4][:, P * j:P * j + P], act_m[s % 2][:, P * j:P * j + P], ident)
                    m.then_inc(moe_full[4], 1)
                    pe.wait_ge(moe_free[4], n + 2)
                    for half in range(2):
                        pe.wait_ge(moe_free[5 + half], n + 1)
                        for j in range(2):
                            m = pe.matmul(bank[5 + half], actT[s % 2][:, j, :], wdn[s][:, j, 512 * half:512 * half + 512], start=(j == 0), stop=(j == 1))
                        m.then_inc(moe_full[5 + half], 1)

        @block.scalar
        def _(act):
            A = act.activation
            act.wait_ge(S["vec_zero"], 1)
            for r, src in vector_rows:
                act.dma_start(vrows[r % P:r % P + src.shape[0], r // P, 0:src.shape[1]], src).then_inc(S["vec_in"], 16)
            act.dma_start(wg.rearrange("p (k c) -> p k c", k=8), w["w_in"][:, 4096:4104].rearrange("(k p) c -> p k c", p=P)).then_inc(S["wg_in"], 16)
            act.dma_start(small[0:4, 200:201], w["igate_b"].rearrange("(h a) -> h a", a=1)).then_inc(S["wg_in"], 16)
            act.dma_start(small[0:4, 201:202], w["fgate_b"].rearrange("(h a) -> h a", a=1)).then_inc(S["wg_in"], 16)

            def root(name):
                sizes, nt, div, kind = NORMS[name]
                n, job, par = len(sizes) * nt, J(name + "s"), list(NORMS).index(name) % 2
                b = see(act, job)
                if kind == "rms":
                    free(A(stat[:, par, 0:n], b[:, 0:n], ACT.Sqrt, bias=eps, scale=1.0 / div), job)
                else:
                    free(A(stat[:, par, 0:n], b[:, 0:n], ACT.Copy, scale=1.0 / div), job)

            highs = [0]

            def panel_highs(upto):
                for n in split_panels[highs[0]:upto]:
                    raw, high, _ = panel_parts(n)
                    act.wait_ge(ring_full[n % SLOTS], 16 * (n // SLOTS + 1))
                    A(high, raw, ACT.Copy).then_inc(S["panel_high"], 1)
                    highs[0] += 1

            def square(dst, src):
                A(dst, src, ACT.Square).then_inc(S["sq_done"], 1)

            def scaled(name, k, n=ND):
                if k < n - 1:
                    act.wait_ge(S["scaled"], SCALED[name] + k + 1)
                else:
                    freed(act, J(RJOB[name]))

            freed(act, J("vec"))
            A(cond, vec[:, COL["c"]:COL["c"] + 8], ACT.Silu).then_inc(S["cond_done"], 1)
            for k in range(ND):
                freed(act, J("xT", k))
                square(sq[:, k, :], xT[:, k, :])
            root("n1")
            act.wait_ge(S["mod_done"], 1)
            for k in range(ND):
                scaled("n1", k)
                A(uT[:, k, :], uT[:, k, :], ACT.Identity, bias=mod[:, k:k + 1]).then_inc(S["shifted"], 1)
            for p in range(4):
                for half in range(2):
                    job = J("glu", 4 * p + 2 + half)
                    b = see(act, job)
                    if p > 0:
                        freed(act, J("glu", 4 * p - 4 + half))
                    free(A(tB[:, half, :], b, ACT.Sigmoid), job)
            act.wait_ge(S["wg_in"], 48)
            free(A(rows["i"], see(act, J("gates", 0))[0:4, :], ACT.Identity, bias=small[0:4, 200:201]), J("gates", 0))
            free(A(rows["f"], see(act, J("gates", 1))[0:4, :], ACT.Identity, bias=small[0:4, 201:202]), J("gates", 1))
            freed(act, J("gates", 1))
            A(rows["e"], rows["f"], ACT.Abs).then_inc(S["gate_act"], 1)
            act.wait_ge(S["gate_act"], 1)
            A(rows["e"], rows["e"], ACT.Exp, scale=-1.0).then_inc(S["gate_act"], 1)
            act.wait_ge(S["gate_act"], 2)
            A(rows["e"], rows["e"], ACT.Ln, bias=1.0).then_inc(S["gate_act"], 1)
            for j in range(16):
                b = see(act, J("qk", j))
                A(qk[:, j, :], b, ACT.Identity, bias=cv("qk_conv_b", j), scale=cv("qk_conv_w", 16 * (QC - 1) + j)).then_inc(S["qk_affine"], 1)
                if j == 0:
                    act.wait_ge(S["gate_dve"], GD_M)
                    A(rows["em"], rows["m"], ACT.Exp, scale=-1.0).then_inc(S["gate_act"], 1)
                freed(act, J("qk", j))
                A(qk[:, j, :], qk[:, j, :], ACT.Silu).then_inc(S["qk_done"], 1)
            act.wait_ge(S["vone_done"], 1)
            for j in range(8):
                b = see(act, J("v", j))
                free(A(v1[:, 2 * (j % 2):2 * (j % 2) + 2, j // 2, 0:HD], b.rearrange("p (t e) -> p t e", t=2), ACT.Copy), J("v", j))
            for j in range(8):
                b = see(act, J("o", j))
                free(A(og[:, 2 * (j % 2):2 * (j % 2) + 2, HD * (j // 2):HD * (j // 2) + HD], b.rearrange("p (t e) -> p t e", t=2), ACT.Sigmoid), J("o", j))
            for h in range(NH):
                for s in range(NT):
                    if s < NT - 1:
                        act.wait_ge(S["w_sub"], (NT - 1) * h + s + 1)
                    else:
                        freed(act, J(f"Mb{h}"))
                    A(tA[:, s, 0:T - P * s], tA[:, s, 0:T - P * s], ACT.Exp, scale=-1.0).then_inc(S["w_exp"], 1)
                if h == 2:
                    root("lm")
            for k in range(ND):
                if k < ND - 1:
                    act.wait_ge(S["lv_sub"], k + 1)
                else:
                    freed(act, J("lmr"))
                if k % NT == 0:
                    see(act, J(f"N{2 + k // NT}", NT - 1))
                square(sq[:, k, :], yc[:, k, :])
            root("lv")
            for k in range(ND):
                scaled("lv", k)
                A(yc[:, k, :], yc[:, k, :], ACT.Silu, bias=cv("cv_ln_b", k)).then_inc(S["lv_done"], 1)
            for t in range(NT):
                for h in range(NH):
                    freed(act, J(f"N{h}", t))
                    i = NH * t + h
                    if i >= 8:
                        act.wait_ge(S["h_sq"], i - 7)
                    A(tA[:, i % 4, HD * (i // 4 % 2):HD * (i // 4 % 2) + HD], hn[:, t, HD * h:HD * h + HD], ACT.Square, accum_out=ssq[:, 4 * t + h:4 * t + h + 1]).then_inc(S["h_sq"], 1)
            act.wait_ge(S["h_chain"], 5)
            A(t16, t16, ACT.Sqrt, bias=eps, scale=1.0 / HD).then_inc(S["h_sq"], 1)
            for k in range(ND):
                b = see(act, J("hT", k))
                free(A(hT[:, k, :], b, ACT.Copy, scale=cv("ml_norm_g", k)), J("hT", k))

            def linear_out(name):
                for k in range(ND):
                    if name == "down":
                        panel_highs(44 + 3 * k + 6)
                    b = see(act, J(name, k))
                    square(sq[:, k, :], b)
                    free(A(uT[:, k, :], b, ACT.Copy), J(name, k))

            linear_out("wo")
            root("n2")
            act.dma_start(posI, w["positions_2"].partition_broadcast(P)).then_inc(S["pos_in"], 16)
            for k in range(ND):
                act.wait_ge(S["x_upd"], k + 1)
                square(sq[:, k, :], xT[:, k, :])
            root("n3")
            panel_highs(4)
            act.wait_ge(S["mod_done"], 2)
            for k in range(ND):
                scaled("n3", k)
                A(uH[:, k, :], uT[:, k, :], ACT.Identity, bias=mod[:, 24 + k:25 + k]).then_inc(S["shifted"], 1)
            for i in range(4):
                act.wait_ge(S["trig_dve"], i + 1)
                A(trig[:, i, :], tA[:, 2 + i % 2, :], ACT.Sin).then_inc(S["trig_act"], 1)
                panel_highs(5 + i)
            act.wait_ge(S["trig_act"], 4)
            def f_high(p):
                for half in range(2):
                    act.wait_ge(S["f_done"], 2 * p + half + 1)
                    A(fH[:, 2 * p + half, :], fT[:, 2 * p + half, :], ACT.Copy).then_inc(S["f_high"], 1)

            for p in range(11):
                if p > 0:
                    f_high(p - 1)
                for j, half in ((0, 0), (0, 1), (1, 0), (1, 1)):
                    panel_highs(max(8, 4 * p + 2 * j + half + 3))
                    b = see(act, J("up", 4 * p + 2 * j + half))
                    c = NF * j + 2 * p + half
                    A(tA[:, 2 * j + half, :], b, ACT.Identity, bias=cv("ffn_conv_b", c), scale=cv("ffn_conv_w", 2 * NF * (FC - 1) + c)).then_inc(S["up_affine"], 1)
                for half in range(2):
                    freed(act, J("up", 4 * p + 2 + half))
                    A(tA[:, 2 + half, :], tA[:, 2 + half, :], ACT.Silu).then_inc(S["up_silu"], 1)
            f_high(10)
            linear_out("down")
            root("n4")
            act.dma_start(memTM, w["mem_2"].rearrange("(m p) d -> p m d", p=P)).then_inc(S["mem_in"], 16)
            for k in range(ND):
                act.wait_ge(S["x_upd"], ND + k + 1)
                square(sq[:, k, :], xT[:, k, :])
            root("n5")
            for j in range(2):
                square(sq[:, j, :], see(act, J("cq", j)))
            square(sq[:, 2, :], see(act, J("ckv")))
            square(cat[0:ROPE, 4, :], see(act, J("kpe"))[0:ROPE, :])
            root("cq")
            root("ck")
            for h in range(NH):
                square(sq[:, h, :], see(act, J("qn", h)))
            for h in range(NH):
                square(sq[0:ROPE, 4 + h, :], see(act, J("qr", h))[0:ROPE, :])
            for h in range(NH):
                square(cat[:, h, :], see(act, J("kn", h)))
            for t in range(NT):
                free(A(mv[:, t, :], see(act, J("mv", t)), ACT.Copy), J("mv", t))
            root("q")
            root("k")

            act.wait_ge(S["zeros_made"], 1)
            act.dma_start(y_dram[2 * T:NB * P, :].rearrange("(p b) (q c) -> p (b q) c", p=P, c=256),
                          zeros.unsqueeze(1).to_broadcast([P, 4 * (NB - 2 * T // P), 256])).then_inc(S["y_zeroed"], 16)

            def exps(name, n, dst, base):
                for t in range(NT):
                    job = J(name, t)
                    act.wait_ge(S["att_max"], base + t + 1)
                    width = n or P * (t + 1)
                    free(A(dst[:, t, 0:width], bank[job.bank][:, 0:width], ACT.Exp, bias=soft[:, 0, base + t:base + t + 1],
                           accum_out=soft[:, 1, base + t:base + t + 1]), job)

            for h in range(NH + 1):
                if h < NH:
                    if h >= 2:
                        see(act, J(f"AT{h - 2}", 3))
                    exps(f"A{h}", 0, att[h % 2], NT * h)
                if h > 0:
                    g = h - 1
                    if g >= 2:
                        see(act, J(f"AO{g - 2}"))
                    for s in range(NT):
                        b = see(act, J(f"AT{g}", s))
                        free(A(attT[g % 2][:, s, P * s:T], b[:, P * s:T], ACT.Copy), J(f"AT{g}", s))
                    free(A(cat[:, g, :], see(act, J(f"AO{g}")), ACT.Copy), J(f"AO{g}"))
            act.dma_start(decay, w["const"][:, CW:CW + 2048].rearrange("p (h t) -> p h t", h=NH)).then_inc(S["decay_in"], 16)
            for t in range(4):
                free(A(rv[:, 2 * (t % 2):2 * (t % 2) + 2, 256 * (t // 2):256 * (t // 2) + 256], see(act, J("rv", t)).rearrange("p (t e) -> p t e", t=2), ACT.Copy), J("rv", t))
            for h in range(NH):
                free(A(rg[:, h, :], see(act, J("rg", h)), ACT.Silu), J("rg", h))
            root("gm")
            for h in range(NH):
                freed(act, J("gmr", h))
                square(sq[:, h, :], cat[:, 4 + h, :])
            root("gv")
            for k in range(ND):
                freed(act, J("wo2", k))
                square(sq[:, k, :], xT[:, k, :])
            root("n6")
            act.dma_start(wr[:, :, 0:NG], w["router_w_group_2"].rearrange("(k p) c -> p k c", p=P)).then_inc(S["rt_in"], 16)
            act.dma_start(wr[:, :, NG:NG + NE], w["router_w_expert_2"].rearrange("(k p) c -> p k c", p=P)).then_inc(S["rt_in"], 16)
            act.dma_start(bias_row[:, 0:NG], w["router_b_group_2"].unsqueeze(0)).then_inc(S["rt_in"], 16)
            act.dma_start(bias_row[:, NG:NG + NE], w["router_b_expert_2"].unsqueeze(0)).then_inc(S["rt_in"], 16)
            for kk in range(4):
                free(A(memT[:, 2 * kk:2 * kk + 2, :], see(act, J("memT", kk)).rearrange("p (k t) -> p k t", k=2), ACT.Copy), J("memT", kk))
            for k in range(ND):
                freed(act, J("memT", k // 2))
                square(sq[:, k, 0:MEM], memT[:, k, :])
            root("nm")
            for k in range(ND):
                square(sq[:, k, :], see(act, J("xq", k)))
            for k in range(ND):
                square(xksq[:, k, :], see(act, J("xk", k))[:, 0:MEM])
            for p in range(4):
                free(A(xv[:, :, 256 * p:256 * p + 256], see(act, J("xv", p)).rearrange("p (t e) -> p t e", t=2), ACT.Copy), J("xv", p))
            root("xq")
            root("xk")
            for h in range(NH + 1):
                if h < NH:
                    if h >= 2:
                        see(act, J(f"XT{h - 2}", 1))
                    exps(f"X{h}", MEM, xp[h % 2], 16 + NT * h)
                if h > 0:
                    g = h - 1
                    if g >= 2:
                        see(act, J(f"XO{g - 2}", 1))
                    for s in range(NM):
                        free(A(xpT[g % 2][:, s, :], see(act, J(f"XT{g}", s)), ACT.Copy), J(f"XT{g}", s))
                    for half in range(2):
                        free(A(xoT[:, 2 * g + half, :], see(act, J(f"XO{g}", half)), ACT.Copy), J(f"XO{g}", half))
            for k in range(ND):
                freed(act, J("xo", k))
                square(sq[:, k, :], xT[:, k, :])
            root("n7")
            act.wait_ge(S["route_dve"], mark["group"])
            A(r_x, r_x, ACT.Exp).then_inc(S["route_act"], 1)
            act.wait_ge(S["route_dve"], mark["expert"])
            A(r_y, r_y, ACT.Exp).then_inc(S["route_act"], 1)
            for j in range(8):
                free(A(hmTM[:, j // 2, 512 * (j % 2):512 * (j % 2) + 512], see(act, J("hmT", j)), ACT.Copy), J("hmT", j))
            for j in range(8):
                freed(act, J("hmT", j))
            act.dma_start(hm_dram.rearrange("(t p) d -> p t d", p=P), hmTM).then_inc(S["hm_out"], 16)
            for j in range(8):
                free(A(xoutTM[:, j // 2, 512 * (j % 2):512 * (j % 2) + 512], see(act, J("xTM", j)), ACT.Copy), J("xTM", j))
            act.wait_ge(S["hm_out"], 16)
            act.wait_ge(S["y_zeroed"], 16)
            for b in range(2):
                act.sem_inc(y_out[b], 16)

            def act_turn(s, n):
                act.wait_ge(moe_full[0], n + 1)
                A(xgT[s % 2][:, 0:4, :], bank[0].rearrange("p (k t) -> p k t", k=4), ACT.Copy).then_inc(moe_free[0], 1)

            act_turn(0, 0)
            for i in rep(act, turns_of(act)):
                for s in range(SLOTS):
                    n = i * SLOTS + s
                    act.wait_ge(moe_full[2 + s % 2], i * 2 + s // 2 + 1)
                    A(act_f[s % 2], bank[2 + s % 2][:, 0:EF], ACT.Silu).then_inc(S["g_silu"], 1)
                    act_turn(s + 1, n + 1)
                    act.wait_ge(moe_full[5], n + 1)
                    act.wait_ge(y_out[s % 2], 16 * (i * 2 + s // 2 + 1))
                    A(yb[s % 2][:, 0:512], bank[5], ACT.Copy).then_inc(moe_free[5], 1)
                    act.wait_ge(moe_free[5], n + 2)
                    act.wait_ge(moe_free[6], n + 2)
                    act.dma_start(y_dram[bass.ds(n * P, P), :], yb[s % 2]).then_inc(y_out[s % 2], 16)
            for t in range(NT):
                act.wait_ge(S["out_sum"], 2 * t + 2)
                act.dma_start(out[P * t:P * t + P, :], xoutTM[:, t, :]).then_inc(S["out_done"], 16)
            act.wait_ge(S["out_done"], 16 * NT)


def kernel(**inputs):
    import concourse.bacc as bacc
    from concourse.bass_utils import run_bass_kernel_spmd

    nc = bacc.Bacc("TRN2", target_bir_lowering=False, num_devices=1)
    arrays, handles = {}, {}
    for name, value in inputs.items():
        a = np.ascontiguousarray(np.asarray(value)[0])
        arrays["in_" + name] = a
        handles[name] = nc.dram_tensor("in_" + name, a.shape, mybir.dt.from_np(a.dtype), kind="ExternalInput").ap()
    arrays["in_const"] = constants()
    handles["const"] = nc.dram_tensor("in_const", arrays["in_const"].shape, F32, kind="ExternalInput").ap()
    out = nc.dram_tensor("out_0", (T, D), F32, kind="ExternalOutput").ap()
    program(nc, handles, out)
    result = run_bass_kernel_spmd(nc, [arrays], core_ids=[0])
    return result.results[0]["out_0"].reshape(1, T, D)
```
